# Optimizing a Trainium2 kernel written in Bass

```python
import math
import numpy as np
import jax
import jax.numpy as jnp
from jax import lax

D_MODEL = 1024
BATCH = 1
SEQ = 512
DEPTH = 2

BRANCH_WIDTH = 512
N_BRANCH = 4
CONV_WIDTH = BRANCH_WIDTH
CONV_K = 3
RET_HEADS = 4
RET_DK = 64
RET_DV = 128
RET_CHUNK = 128
RET_THETA = 10000.0
SGU_GROUPS = 4
SGU_GROUP_DIM = BRANCH_WIDTH // SGU_GROUPS
SGU_CHUNK = 128
SGU_WIDTH = BRANCH_WIDTH
DIFF_HEADS = 4
DIFF_HEAD_DIM = 64
DIFF_V_DIM = 2 * DIFF_HEAD_DIM
Q_BLOCK = 128
ROPE_THETA = 500000.0
ROT_DIM = DIFF_HEAD_DIM // 4
CONV_COLS = 3 * CONV_WIDTH
RET_COLS = 2 * RET_HEADS * RET_DK + 2 * RET_HEADS * RET_DV
SGU_COLS = 2 * SGU_WIDTH
DIFF_COLS = 2 * DIFF_HEADS * 2 * DIFF_HEAD_DIM + DIFF_HEADS * DIFF_V_DIM
IN_COLS = CONV_COLS + RET_COLS + SGU_COLS + DIFF_COLS
N_EXPERTS = 16
N_GROUPS = 4
EXPERTS_PER_GROUP = N_EXPERTS // N_GROUPS
TOP_K = 2
D_EXPERT = 1024
MOE_BLOCK = 128
ALPHA = (2.0 * DEPTH) ** 0.25
BETA = (8.0 * DEPTH) ** -0.25
LN_EPS = 1e-5
RMS_EPS = 1e-6

kernel_name = "hybrid_gated_parallel_mixers_deepnorm_moe"

def layer_norm(x, g, b):
    xf = x.astype(jnp.float32)
    mu = jnp.mean(xf, axis=-1, keepdims=True)
    var = jnp.mean(jnp.square(xf - mu), axis=-1, keepdims=True)
    y = (xf - mu) * lax.rsqrt(var + LN_EPS) * g.astype(jnp.float32) + b.astype(jnp.float32)
    return y.astype(x.dtype)

def rms_norm(x):
    xf = x.astype(jnp.float32)
    return xf * lax.rsqrt(jnp.mean(jnp.square(xf), axis=-1, keepdims=True) + RMS_EPS)

def rotary(x, pos, rot_dim, theta):
    half = rot_dim // 2
    inv_freq = theta ** (-jnp.arange(half, dtype=jnp.float32) / half)
    ang = pos.astype(jnp.float32)[..., None] * inv_freq
    ang = ang.reshape(ang.shape[:2] + (1,) * (x.ndim - 3) + (half,))
    cos, sin = jnp.cos(ang), jnp.sin(ang)
    xr = x[..., :rot_dim].astype(jnp.float32)
    x1, x2 = xr[..., :half], xr[..., half:]
    rot = jnp.concatenate([x1 * cos - x2 * sin, x2 * cos + x1 * sin], axis=-1).astype(x.dtype)
    return jnp.concatenate([rot, x[..., rot_dim:]], axis=-1)

def short_conv_mixer(z, conv_w):
    b_gate, c_gate, u = jnp.split(z, 3, axis=-1)
    y = lax.conv_general_dilated(
        c_gate * u, conv_w.astype(z.dtype), window_strides=(1,), padding=[(CONV_K - 1, 0)],
        dimension_numbers=("NWC", "WIO", "NWC"), feature_group_count=CONV_WIDTH)
    return b_gate * y

def retention_mixer(z, pos):
    bsz, seq, _ = z.shape
    hk, hv = RET_HEADS * RET_DK, RET_HEADS * RET_DV
    q, k, v, g = jnp.split(z, [hk, 2 * hk, 2 * hk + hv], axis=-1)
    q = rotary(q.reshape(bsz, seq, RET_HEADS, RET_DK), pos, RET_DK, RET_THETA).astype(jnp.float32)
    k = rotary(k.reshape(bsz, seq, RET_HEADS, RET_DK), pos, RET_DK, RET_THETA).astype(jnp.float32)
    k = k * (RET_DK ** -0.5)
    v = v.reshape(bsz, seq, RET_HEADS, RET_DV).astype(jnp.float32)
    log_gamma = jnp.log1p(-jnp.exp2(-5.0 - jnp.arange(RET_HEADS, dtype=jnp.float32)))
    c, n = RET_CHUNK, seq // RET_CHUNK
    qc = q.reshape(bsz, n, c, RET_HEADS, RET_DK)
    kc = k.reshape(bsz, n, c, RET_HEADS, RET_DK)
    vc = v.reshape(bsz, n, c, RET_HEADS, RET_DV)
    idx = jnp.arange(c, dtype=jnp.float32)
    rel = idx[:, None] - idx[None, :]
    decay = jnp.where(rel >= 0, jnp.exp(jnp.maximum(rel, 0.0)[None] * log_gamma[:, None, None]), 0.0)
    scores = jnp.einsum("bnihd,bnjhd->bnhij", qc, kc) * decay
    inner = jnp.einsum("bnhij,bnjhe->bnihe", scores, vc)
    k_decay = jnp.exp((c - 1 - idx)[:, None] * log_gamma[None, :])
    kv = jnp.einsum("bnjhd,bnjhe->bnhde", kc * k_decay[:, :, None], vc)
    chunk_decay = jnp.exp(c * log_gamma)[None, :, None, None]

    def step(state, kv_n):
        return state * chunk_decay + kv_n, state

    _, prev = lax.scan(step, jnp.zeros((bsz, RET_HEADS, RET_DK, RET_DV), jnp.float32),
                       jnp.moveaxis(kv, 1, 0))
    prev = jnp.moveaxis(prev, 0, 1)
    q_decay = jnp.exp((idx + 1.0)[:, None] * log_gamma[None, :])
    cross = jnp.einsum("bnihd,bnhde->bnihe", qc * q_decay[:, :, None], prev)
    o = rms_norm((inner + cross).reshape(bsz, seq, RET_HEADS, RET_DV))
    gate = jax.nn.silu(g.reshape(bsz, seq, RET_HEADS, RET_DV).astype(jnp.float32))
    return (gate * o).reshape(bsz, seq, RET_HEADS * RET_DV).astype(z.dtype)

def spatial_gating_mixer(z, ln_g, ln_b, w_s, b_s):
    bsz, seq, _ = z.shape
    u, v = jnp.split(z, 2, axis=-1)
    v = layer_norm(v, ln_g, ln_b)
    n = seq // SGU_CHUNK
    v = v.reshape(bsz, n, SGU_CHUNK, SGU_GROUPS, SGU_GROUP_DIM)
    w = jnp.tril(w_s).astype(z.dtype)
    s = jnp.einsum("gts,bnsgc->bntgc", w, v) + b_s.T.astype(z.dtype)[None, None, :, :, None]
    return u * s.reshape(bsz, seq, SGU_WIDTH)

def diff_attention_mixer(z, pos, lq1, lk1, lq2, lk2, subln_g, lambda_init):
    bsz, seq, _ = z.shape
    hq = DIFF_HEADS * 2 * DIFF_HEAD_DIM
    q, k, v = jnp.split(z, [hq, 2 * hq], axis=-1)
    q = q.reshape(bsz, seq, DIFF_HEADS, 2, DIFF_HEAD_DIM)
    k = k.reshape(bsz, seq, DIFF_HEADS, 2, DIFF_HEAD_DIM)
    v = v.reshape(bsz, seq, DIFF_HEADS, DIFF_V_DIM)
    q = rotary(q, pos, ROT_DIM, ROPE_THETA) * (DIFF_HEAD_DIM ** -0.5)
    k = rotary(k, pos, ROT_DIM, ROPE_THETA)
    lam = (jnp.exp(jnp.sum(lq1.astype(jnp.float32) * lk1.astype(jnp.float32)))
           - jnp.exp(jnp.sum(lq2.astype(jnp.float32) * lk2.astype(jnp.float32))) + lambda_init)
    n = seq // Q_BLOCK
    qb = jnp.moveaxis(q.reshape(bsz, n, Q_BLOCK, DIFF_HEADS, 2, DIFF_HEAD_DIM), 1, 0)
    key_idx = jnp.arange(seq)

    def block(args):
        q_blk, blk = args
        s = jnp.einsum("bqhcd,bkhcd->bhcqk", q_blk, k).astype(jnp.float32)
        q_idx = blk * Q_BLOCK + jnp.arange(Q_BLOCK)
        s = jnp.where(key_idx[None, :] <= q_idx[:, None], s, -jnp.inf)
        p = jax.nn.softmax(s, axis=-1)
        a = p[:, :, 0] - lam * p[:, :, 1]
        return jnp.einsum("bhqk,bkhe->bqhe", a.astype(v.dtype), v)

    o = lax.map(block, (qb, jnp.arange(n)))
    o = jnp.moveaxis(o, 0, 1).reshape(bsz, seq, DIFF_HEADS, DIFF_V_DIM)
    o = rms_norm(o) * subln_g.astype(jnp.float32) * (1.0 - lambda_init)
    return o.reshape(bsz, seq, DIFF_HEADS * DIFF_V_DIM).astype(z.dtype)

def route(xf, w_router, b_router):
    scores = jax.nn.softmax((xf @ w_router).astype(jnp.float32), axis=-1)
    sel = scores + b_router.astype(jnp.float32)
    grp_score = jnp.sum(lax.top_k(sel.reshape(-1, N_GROUPS, EXPERTS_PER_GROUP), TOP_K)[0], axis=-1)
    best = jnp.argmax(grp_score, axis=-1)
    expert_group = jnp.arange(N_EXPERTS) // EXPERTS_PER_GROUP
    masked = jnp.where(expert_group[None, :] == best[:, None], sel, -jnp.inf)
    _, idx = lax.top_k(masked, TOP_K)
    w = jnp.take_along_axis(scores, idx, axis=-1)
    return idx, w / jnp.sum(w, axis=-1, keepdims=True)

def moe_ffn(h, w_router, b_router, w1, w3, w2):
    bsz, seq, d = h.shape
    xf = h.reshape(-1, d)
    t = xf.shape[0]
    idx, gw = route(xf, w_router, b_router)
    a = t * TOP_K
    flat_e = idx.reshape(-1)
    order = jnp.argsort(flat_e)
    sorted_e = flat_e[order]
    tok = order // TOP_K
    counts = jnp.bincount(flat_e, length=N_EXPERTS)
    padded = ((counts + MOE_BLOCK - 1) // MOE_BLOCK) * MOE_BLOCK
    pad_end = jnp.cumsum(padded)
    pad_start = pad_end - padded
    start = jnp.cumsum(counts) - counts
    dest = pad_start[sorted_e] + (jnp.arange(a) - start[sorted_e])
    n_rows = a + N_EXPERTS * MOE_BLOCK
    n_blk = n_rows // MOE_BLOCK
    buf = jnp.zeros((n_rows, d), xf.dtype).at[dest].set(xf[tok])
    blk_e = jnp.minimum(jnp.searchsorted(pad_end, jnp.arange(n_blk) * MOE_BLOCK, side="right"),
                        N_EXPERTS - 1)

    def expert_block(args):
        xb, e = args
        return (jax.nn.silu(xb @ w1[e]) * (xb @ w3[e])) @ w2[e]

    out = lax.map(expert_block, (buf.reshape(n_blk, MOE_BLOCK, d), blk_e)).reshape(n_rows, d)
    contrib = out[dest] * gw.reshape(-1)[order][:, None].astype(xf.dtype)
    y = jnp.zeros((t, d), xf.dtype).at[tok].add(contrib)
    return y.reshape(bsz, seq, d)

def setup_inputs(seed: int = 0) -> dict:
    key = jax.random.key(seed)
    ks = jax.random.split(key, 32)
    nrm = lambda k, shape, s: jax.random.normal(k, shape, jnp.float32) * s
    gain = lambda k, shape: 1.0 + 0.05 * jax.random.normal(k, shape, jnp.float32)
    L, D, W = DEPTH, D_MODEL, BRANCH_WIDTH
    positions = (jnp.arange(SEQ, dtype=jnp.int32)[None, :]
                 + jax.random.randint(ks[1], (BATCH, 1), 0, 4096, dtype=jnp.int32))
    return {
        "x": nrm(ks[0], (BATCH, SEQ, D), 1.0),
        "positions": positions,
        "ln_in_g": gain(ks[2], (D,)),
        "ln_in_b": nrm(ks[3], (D,), 0.05),
        "w_in": nrm(ks[4], (L, D, IN_COLS), D ** -0.5),
        "conv_w": nrm(ks[5], (L, CONV_K, 1, CONV_WIDTH), CONV_K ** -0.5),
        "sgu_ln_g": gain(ks[6], (L, SGU_WIDTH)),
        "sgu_ln_b": nrm(ks[7], (L, SGU_WIDTH), 0.05),
        "w_s": nrm(ks[8], (L, SGU_GROUPS, SGU_CHUNK, SGU_CHUNK), SGU_CHUNK ** -0.5),
        "b_s": gain(ks[9], (L, SGU_GROUPS, SGU_CHUNK)),
        "lambda_q1": nrm(ks[10], (L, DIFF_HEAD_DIM), 0.1),
        "lambda_k1": nrm(ks[11], (L, DIFF_HEAD_DIM), 0.1),
        "lambda_q2": nrm(ks[12], (L, DIFF_HEAD_DIM), 0.1),
        "lambda_k2": nrm(ks[13], (L, DIFF_HEAD_DIM), 0.1),
        "diff_subln_g": gain(ks[14], (L, DIFF_V_DIM)),
        "w_gate": nrm(ks[15], (L, N_BRANCH, D, D), D ** -0.5),
        "b_gate": nrm(ks[16], (L, N_BRANCH, D), 0.05),
        "w_branch": nrm(ks[17], (L, N_BRANCH, W, D), BETA * W ** -0.5),
        "w_o": nrm(ks[18], (L, D, D), BETA * D ** -0.5),
        "ln1_g": gain(ks[19], (L, D)),
        "ln1_b": nrm(ks[20], (L, D), 0.05),
        "w_router": nrm(ks[21], (D, N_EXPERTS), D ** -0.5),
        "b_router": nrm(ks[22], (N_EXPERTS,), 0.01),
        "w1": nrm(ks[23], (L, N_EXPERTS, D, D_EXPERT), D ** -0.5),
        "w3": nrm(ks[24], (L, N_EXPERTS, D, D_EXPERT), D ** -0.5),
        "w2": nrm(ks[25], (L, N_EXPERTS, D_EXPERT, D), BETA * D_EXPERT ** -0.5),
        "ln2_g": gain(ks[26], (L, D)),
        "ln2_b": nrm(ks[27], (L, D), 0.05),
    }

def reference(x, positions, ln_in_g, ln_in_b, w_in, conv_w, sgu_ln_g, sgu_ln_b, w_s, b_s,
              lambda_q1, lambda_k1, lambda_q2, lambda_k2, diff_subln_g, w_gate, b_gate,
              w_branch, w_o, ln1_g, ln1_b, w_router, b_router, w1, w3, w2, ln2_g, ln2_b):
    split_at = [CONV_COLS, CONV_COLS + RET_COLS, CONV_COLS + RET_COLS + SGU_COLS]
    h = layer_norm(x, ln_in_g, ln_in_b)
    for l in range(DEPTH):
        z = h @ w_in[l]
        z_conv, z_ret, z_sgu, z_diff = jnp.split(z, split_at, axis=-1)
        lambda_init = 0.8 - 0.6 * math.exp(-0.3 * l)
        branches = (
            short_conv_mixer(z_conv, conv_w[l]),
            retention_mixer(z_ret, positions),
            spatial_gating_mixer(z_sgu, sgu_ln_g[l], sgu_ln_b[l], w_s[l], b_s[l]),
            diff_attention_mixer(z_diff, positions, lambda_q1[l], lambda_k1[l], lambda_q2[l],
                                 lambda_k2[l], diff_subln_g[l], lambda_init),
        )
        merged = jnp.zeros_like(h)
        for g, y in enumerate(branches):
            gate = jax.nn.sigmoid(h @ w_gate[l, g] + b_gate[l, g])
            merged = merged + gate * (y @ w_branch[l, g])
        h = layer_norm(ALPHA * h + merged @ w_o[l], ln1_g[l], ln1_b[l])
        h = layer_norm(ALPHA * h + moe_ffn(h, w_router, b_router, w1[l], w3[l], w2[l]),
                       ln2_g[l], ln2_b[l])
    return h


_drawn_inputs = setup_inputs


def setup_inputs(seed=0):
    import zlib

    import numpy as np

    out = dict(_drawn_inputs(seed))
    spreads = {}
    factors = {'sgu_ln_g': 4.767,
     'sgu_ln_b': 8.0,
     'b_s': 3.899,
     'lambda_q1': 4.22,
     'lambda_k1': 5.118,
     'diff_subln_g': 4.152,
     'b_gate': 5.005,
     'lambda_q2': 8.0,
     'lambda_k2': 3.739}
    for name, (base, spread) in spreads.items():
        noise = np.random.default_rng([zlib.crc32(name.encode()), seed]).standard_normal(out[name].shape)
        drawn = base * np.exp(spread * noise) if base else spread * noise
        out[name] = jnp.asarray(drawn.astype(out[name].dtype))
    for name, factor in factors.items():
        out[name] = (out[name] * factor).astype(out[name].dtype)
    return out
```

```python
import math
from contextlib import ExitStack

import numpy as np
import concourse.bass as bass
from concourse import mybir
from concourse.alu_op_type import AluOpType as ALU

F32 = mybir.dt.float32
F32R = mybir.dt.float32r
I32 = mybir.dt.int32
ACT = mybir.ActivationFunctionType
AX = mybir.AxisListType.X

P = 128
D = 1024
T = 512
DEPTH = 2
KD = D // P
TT = T // P
W = 512
IN_COLS = 11 * W
E = 16
EG = 4
NG = 4
OVF = 7
NBLK = E + OVF + 1
ALPHA = (2.0 * DEPTH) ** 0.25
LN_EPS = 1e-5
RMS_EPS = 1e-6
NEG = -1e30
TWO_PI = 2 * math.pi

CONST = {}


def _const_layout():
    at = 0
    for name, n in (("ident", 128), ("swap_ret", 128), ("swap_diff", 128), ("upper", 128), ("strict", 128),
                    ("ones", 128), ("freq_ret", 1), ("freq_diff", 1), ("first_e", E), ("first_g", NG),
                    ("row0", E), ("block", NBLK), ("own", NBLK), ("lam", 2 * DEPTH), ("eps", 2)):
        CONST[name] = (at, at + n)
        at += n
    return at


NCONST = _const_layout()


def constants():
    c = np.zeros((P, NCONST), np.float32)

    def put(name, value):
        a, b = CONST[name]
        c[:, a:b] = value

    p = np.arange(P)
    put("ident", np.eye(P))
    for name, head, rot in (("swap_ret", 64, 64), ("swap_diff", 64, 16)):
        s = np.zeros((P, P))
        for m in range(P):
            d = m % head
            if d < rot // 2:
                s[m + rot // 2, m] = -1.0
            elif d < rot:
                s[m - rot // 2, m] = 1.0
        put(name, s)
    put("upper", p[None, :] >= p[:, None])
    put("strict", p[None, :] > p[:, None])
    put("ones", 1.0)
    f = np.float32
    inv_r = np.power(f(10000.0), -np.arange(32, dtype=f) / f(32)).astype(f)
    inv_d = np.power(f(500000.0), -np.arange(8, dtype=f) / f(8)).astype(f)
    put("freq_ret", inv_r[(p % 64) % 32][:, None])
    put("freq_diff", np.where(p % 64 < 16, inv_d[(p % 64) % 8], 0)[:, None])
    put("first_e", E - np.arange(E))
    put("first_g", NG - np.arange(NG))
    put("row0", P * np.arange(E))
    put("block", np.arange(NBLK) - E)
    b = np.arange(NBLK)
    put("own", np.where(b < E, b, 0))
    lam = []
    for l in range(DEPTH):
        li = 0.8 - 0.6 * math.exp(-0.3 * l)
        lam += [li, 1.0 - li]
    put("lam", np.array(lam))
    put("eps", np.array([LN_EPS, RMS_EPS]))
    x = np.arange(T)
    mask = np.zeros((P, T), np.float32)
    mask[:, T - P:] = np.where(p[None, :] > p[:, None], NEG, 0.0)
    decay = np.zeros((4, P, T), np.float32)
    for h in range(4):
        lg = np.float32(np.log1p(-np.exp2(np.float32(-5.0 - h))))
        rel = (x[None, :] - p[:, None]).astype(np.float32)
        decay[h] = np.where(rel >= 0, np.exp(np.maximum(rel, 0) * lg) * 0.125, 0.0)
    return c, mask, decay


CONV, DIFF, RET, SGU = 0, 3, 1, 2
GROUPS = {
    CONV: [("T", 0), ("T", 1), ("T", 2)],
    DIFF: [("T", 8), ("T", 9), ("N", 10)],
    RET: [("T", 3), ("N", 4), ("T", 5)],
    SGU: [("T", 6), ("N", 7)],
}
ZBUF = {CONV: 1, DIFF: 0, RET: 1, SGU: 0}
ORDER = [CONV, DIFF, RET, SGU]


def dense_plan():
    chunks = []

    def project(b):
        for g, (kind, tile) in enumerate(GROUPS[b]):
            for half in range(2):
                chunks.append(dict(kind="Z" + kind, b=b, g=g, tile=tile, half=half, units=[]))

    def gates(b):
        for q in range(4):
            chunks.append(dict(kind="gate", b=b, q=q, units=[]))
            chunks.append(dict(kind="branch", b=b, q=q, units=[]))

    project(CONV)
    project(DIFF)
    gates(CONV)
    project(RET)
    gates(DIFF)
    project(SGU)
    gates(RET)
    gates(SGU)
    for n in range(2):
        for half in range(2):
            chunks.append(dict(kind="wo", n=n, half=half, units=[]))

    def where(kind, b):
        return [c for c, x in enumerate(chunks) if x["kind"].startswith(kind) and x.get("b") == b]

    def at(slot, *unit):
        c, end = slot
        chunks[c]["units" if end else "mid"].append(unit)

    def halves(cs):
        return [(c, end) for c in cs for end in (0, 1)]

    for x in chunks:
        x["mid"] = []
    zd, zr, zs = (where("Z", b) for b in (DIFF, RET, SGU))
    gc, gd, gr, gs = (sorted(where("gate", b) + where("branch", b)) for b in ORDER)

    for m in range(4):
        at((zd[m], 1), "conv", m)
    at((gc[0] - 1, 1), "split", CONV)
    at((zd[2], 0), "rotate", DIFF, 0)
    at((zd[4], 0), "rotate", DIFF, 1)
    slots = [(gc[0] - 1, 1)] + halves(gc + zr)[:-1]
    units = 4 * TT
    for u in range(units + 3):
        slot = slots[u * (len(slots) - 1) // (units + 2)]
        if u >= TT + 1 and (u - 1) % TT == 0:
            at(slot, "diff_values", (u - 1) // TT - 1)
        if 0 < u <= units:
            at(slot, "diff_transpose", u - 1)
        if u < units:
            at(slot, "diff_scores", u)
        if u >= TT + 2 and (u - 2) % TT == 0:
            at(slot, "diff_norm", (u - 2) // TT - 1)
    at((gd[0] - 1, 1), "split", DIFF)
    slots = halves(gd + zs)[:-1]
    steps = [("rotate", RET, 0)] + [(k, h) for h in range(4) for k in ("ret_scores", "ret_values", "ret_norm")]
    for s, unit in enumerate(steps):
        at(slots[s * (len(slots) - 1) // (len(steps) - 1)], *unit)
    at((gr[0] - 1, 1), "split", RET)
    at((gr[0], 1), "sgu_mask")
    for n in range(TT):
        at((gr[1 + n], 1), "sgu_norm", n)
    at((gr[6], 0), "sgu_mix")
    at((gs[0] - 1, 1), "split", SGU)
    for q in range(3):
        at((gs[-1], 0), "merge_split", q)
    at((gs[-1], 1), "merge_split", 3)
    return chunks


class Steps:

    def __init__(self, engine, done):
        self.engine, self.done, self.count = engine, done, 0

    def then(self, instruction):
        self.count += 1
        instruction.then_inc(self.done, 1)
        self.engine.wait_ge(self.done, self.count)


def layer_norm_stats(v, order, x, n, stats, mean_var):
    for i in range(n):
        last = v.bn_stats(stats[:, i, :], x[:, i * 512:(i + 1) * 512])
    order.then(last)
    order.then(v.bn_aggr(mean_var, stats[:, 0:n, :].rearrange("p a b -> p (a b)")))


def program(nc, a, out):
    plan = dense_plan()
    nchunk = len(plan)
    c_of = {}
    for c, x in enumerate(plan):
        for unit in x["mid"] + x["units"]:
            c_of[unit] = c

    origin = -(-nc.sbuf_base // 32) * 32
    place = [0]

    def sb(name, shape, dt=F32, at=None):
        size = 4 * int(np.prod(shape[1:]))
        offset = place[0] if at is None else at
        if at is None:
            place[0] += -(-size // 32) * 32
        t = nc.alloc_sbuf_tensor_at(name, shape, dt, offset=origin + offset)
        return t

    consts = sb("consts", [P, NCONST])

    def const(name, rows=P):
        lo, hi = CONST[name]
        return consts[0:rows, lo:hi]

    cos_ret, sin_ret = sb("cos_ret", [P, T]), sb("sin_ret", [P, T])
    cos_diff, sin_diff = sb("cos_diff", [P, T]), sb("sin_diff", [P, T])
    causal = sb("causal", [P, T])
    ln_stats = sb("ln_stats", [P, TT, 2, 6])
    ln_mv = sb("ln_mv", [P, TT, 2])
    small = sb("small", [P, 14])
    ln_sd = small[:, 10:14]
    z0_at = place[0]
    z0 = sb("z0", [P, 3, TT, W])
    h = sb("h", [P, TT, D], at=z0_at)
    shared = place[0]
    z1_at = place[0]
    z1 = sb("z1", [P, 3, TT, W])
    ln1_gb = sb("ln1_gb", [P, 2, D], at=z1_at)
    z = {0: z0, 1: z1}
    hT_head, hT_tail = sb("hT_head", [P, KD, T], F32R), sb("hT_tail", [P, KD, T], F32R)
    merged = sb("merged", [P, KD, T])
    yT_head, yT_tail = sb("yT_head", [P, 4, T], F32R), sb("yT_tail", [P, 4, T], F32R)
    NRAW = 3
    raw = [sb(f"raw{i}", [P, 2048]) for i in range(NRAW)]
    w_head = [sb(f"w_head{i}", [P, 2048], F32R) for i in range(2)]
    w_tail = [sb(f"w_tail{i}", [P, 2048], F32R) for i in range(2)]
    att = sb("att", [P, 2, T])
    attT = sb("attT", [P, TT, T])
    decay = sb("decay", [P, 2, T])
    gate = sb("gate", [P, 2, T])
    square_at = place[0]
    square = sb("square", [P, T])
    std = sb("std", [P, T])
    silu = sb("silu", [P, T])
    prow = sb("prow", [45, P], at=square_at)
    prm = sb("prm", [P, 45])
    lam_rows = sb("lam_rows", [P, 4, 64], at=square_at + 4 * P)
    lam_in, lam, top, rowsum = small[:, 0:2], small[:, 2:6], small[:, 6:8], small[:, 8:10]
    assert origin + place[0] <= nc.sbuf_usable_end, origin + place[0] - nc.sbuf_usable_end

    place[0] = shared
    route = sb("route", [P, 24, TT * E])
    w_router = sb("w_router", [P, KD, E])
    b_router = sb("b_router", [P, E])
    slots_f = sb("slots_f", [P, 2, TT])
    slots = sb("slots", [P, 2, TT], I32)
    share = sb("share", [P, 2, TT])
    count_f = sb("count_f", [P, 4, E])
    over = sb("over", [P, NBLK, E])
    block_f = sb("block_f", [P, NBLK + 1])
    block_i = sb("block_i", [P, NBLK + 1], I32)
    moe_base = place[0]
    hT = sb("hT", [P, KD, T])
    place[0] = moe_base
    NER = 6
    e_raw = [sb(f"e_raw{i}", [P, 4, 512]) for i in range(NER)]
    NEH = 3
    e_head = [sb(f"e_head{i}", [P, 4, 512], F32R) for i in range(NEH)]
    e_tail = [sb(f"e_tail{i}", [P, 4, 512], F32R) for i in range(NEH)]
    x_rows = sb("x_rows", [P, D])
    xT_head, xT_tail = sb("xT_head", [P, KD, P], F32R), sb("xT_tail", [P, KD, P], F32R)
    act_rows = sb("act_rows", [P, 2, 512])
    aT_head, aT_tail = sb("aT_head", [P, KD, P], F32R), sb("aT_tail", [P, KD, P], F32R)
    e_sig = sb("e_sig", [P, 512])
    e_out = sb("e_out", [P, 2, 512])
    assert origin + place[0] <= nc.sbuf_usable_end, origin + place[0] - nc.sbuf_usable_end
    place[0] = moe_base
    rows1 = sb("rows1", [P, TT, D])
    rows2 = sb("rows2", [P, TT, D])
    ln2_gb = sb("ln2_gb", [P, 2, D])

    slot_x = a["slot_x"]
    slot_y = a["slot_y"]

    with ExitStack() as ctx:
        ps = ctx.enter_context(nc.psum_tensor("ps", [P, 8, 512], F32))
        sems = []

        def sem(name):
            s = ctx.enter_context(nc.semaphore(name))
            sems.append(s)
            return s

        in_ready, pos_ready = sem("in_ready"), sem("pos_ready")
        cleared, zeros_ready = sem("cleared"), sem("zeros_ready")
        dve_done, root_done, angle_ready, sin_done = (sem("dve_done"), sem("root_done"), sem("angle_ready"),
                                                      sem("sin_done"))
        stat_ready, normed_ready, stored = sem("stat_ready"), sem("normed_ready"), sem("stored")
        setup_sems = list(sems)
        zeros, gb = z1[:, 0, 0:2, :], z1[:, 1, :, :]
        gbv = z1[:, 1, :, :].rearrange("p a b -> p (a b)").rearrange("p (a b) -> p a b", a=2)
        pos_i = nc.alloc_sbuf_tensor_at("pos_i", [P, T], I32, offset=origin + z1_at + 4 * 4096)
        ang = sb("ang", [P, 2, 2, T], at=z1_at + 4 * 4608)
        turns_i = nc.alloc_sbuf_tensor_at("turns_i", [P, 2, T], I32, offset=origin + z1_at + 4 * 4608 + 4 * 2048)
        turns = sb("turns", [P, 2, T], at=z1_at + 4 * 4608 + 4 * 3072)
        posf = sb("posf", [P, T], at=z1_at + 4 * 4608 + 4 * 4096)

        with nc.Block() as block:
            @block.sync
            def _(sp):
                sp.dma_start(consts[:], a["consts"][:, :]).then_inc(pos_ready, 16)
                sp.dma_start(pos_i[:], a["positions"][0:1, :].to_broadcast((P, T))).then_inc(pos_ready, 16)
                sp.dma_start(causal[:], a["causal"][:, :]).then_inc(pos_ready, 16)
                sp.dma_start(h[:], a["x"][0].rearrange("(t p) d -> p t d", p=P)).then_inc(in_ready, 16)
                for i, name in enumerate(("ln_in_g", "ln_in_b")):
                    sp.dma_start(gbv[:, i, :], a[name].rearrange("(a d) -> a d", a=1).to_broadcast((P, D)))\
                      .then_inc(in_ready, 16)
                sp.wait_ge(zeros_ready, 1)
                for b in range(NBLK):
                    for rows in (slot_x, slot_y):
                        sp.dma_start(rows[b * P:(b + 1) * P, :].rearrange("p (a d) -> p a d", a=2), zeros)\
                          .then_inc(cleared, 16)
                sp.wait_ge(normed_ready, 1)
                sp.dma_start(out[0].rearrange("(t p) d -> p t d", p=P), h[:]).then_inc(stored, 16)
                sp.wait_ge(stored, 16)
                sp.wait_ge(cleared, 32 * NBLK)

            @block.gpsimd
            def _(pool):
                pool.memset(zeros, 0.0).then_inc(zeros_ready, 1)

            @block.scalar
            def _(act):
                act.wait_ge(stat_ready, 1)
                act.activation(ln_sd, ln_mv[:, :, 1], ACT.Sqrt, bias=const("eps")[:, 0:1]).then_inc(root_done, 1)
                act.wait_ge(angle_ready, 1)
                for i, (co, si) in enumerate(((cos_ret, sin_ret), (cos_diff, sin_diff))):
                    act.activation(si[:], ang[:, i, 0, :], ACT.Sin)
                    act.activation(co[:], ang[:, i, 1, :], ACT.Sin).then_inc(sin_done, 1)

            @block.vector
            def _(v):
                order = Steps(v, dve_done)
                v.wait_ge(pos_ready, 48)
                order.then(v.tensor_copy(posf[:], pos_i[:]))
                for i, f in enumerate(("freq_ret", "freq_diff")):
                    last = v.tensor_scalar(ang[:, i, 0, :], posf[:], const(f), None, ALU.mult)
                order.then(last)
                order.then(v.tensor_scalar(turns[:], ang[:, :, 0, :], 1.0 / TWO_PI, None, ALU.mult))
                order.then(v.tensor_copy(turns_i[:], turns[:]))
                order.then(v.tensor_copy(turns[:], turns_i[:]))
                c1 = 6.28125
                c2 = float(np.float32(round((TWO_PI - c1) * 2 ** 20) / 2 ** 20))
                c3 = TWO_PI - c1 - c2
                for c in (c1, c2, c3):
                    order.then(v.scalar_tensor_tensor(out=ang[:, :, 0, :], in0=turns[:], scalar=-c,
                                                      in1=ang[:, :, 0, :], op0=ALU.mult, op1=ALU.add))
                order.then(v.tensor_scalar(ang[:, :, 0, :], ang[:, :, 0, :], 3.1415925, -3.1415925, ALU.min, ALU.max))
                order.then(v.tensor_scalar(ang[:, :, 1, :], ang[:, :, 0, :], -1.0, None, ALU.mult))
                order.then(v.tensor_tensor(ang[:, :, 1, :], ang[:, :, 1, :], ang[:, :, 0, :], ALU.max))
                v.tensor_scalar(ang[:, :, 1, :], ang[:, :, 1, :], -1.0, math.pi / 2, ALU.mult, ALU.add)\
                 .then_inc(angle_ready, 1)
                v.wait_ge(in_ready, 48)
                for t in range(TT):
                    layer_norm_stats(v, order, h[:, t, :], 2, ln_stats[:, t], ln_mv[:, t, :])
                v.engine_nop().then_inc(stat_ready, 1)
                v.wait_ge(root_done, 1)
                order.then(v.reciprocal(ln_sd, ln_sd))
                for t in range(TT):
                    order.then(v.tensor_scalar(h[:, t, :], h[:, t, :], ln_mv[:, t, 0:1], ln_sd[:, t:t + 1],
                                               ALU.subtract, ALU.mult))
                order.then(v.tensor_tensor(h[:], h[:], gbv[:, 0:1, :].to_broadcast((P, TT, D)), ALU.mult))
                v.tensor_tensor(h[:], h[:], gbv[:, 1:2, :].to_broadcast((P, TT, D)), ALU.add)\
                 .then_inc(normed_ready, 1)
                v.wait_ge(sin_done, 2)
        first_layer_sem = len(sems)

        raw_in = [sem(f"raw_in{i}") for i in range(NRAW)]
        heads, tails, chunk_used = sem("heads"), sem("tails"), sem("chunk_used")
        z_moved, gates_done, merged_done = sem("z_moved"), sem("gates_done"), sem("merged_done")
        h_turned, hT_heads, hT_tails = sem("h_turned"), sem("hT_heads"), sem("hT_tails")
        params_in, prm_turned, prm_ready = sem("params_in"), sem("prm_turned"), sem("prm_ready")
        lam_exp_in, lam_exp = sem("lam_exp_in"), sem("lam_exp")
        swapped, rotated = sem("swapped"), sem("rotated")
        scores_ready, masked, exps_done, att_ready = (sem("scores_ready"), sem("masked"), sem("exps_done"),
                                                      sem("att_ready"))
        att_turned, att_copied, values_ready = sem("att_turned"), sem("att_copied"), sem("values_ready")
        squared, summed, rooted, normed = sem("squared"), sem("summed"), sem("rooted"), sem("normed")
        decay_in = [sem("decay_in0"), sem("decay_in1")]
        ret_scores_ready, decayed, ret_values_ready = (sem("ret_scores_ready"), sem("decayed"),
                                                       sem("ret_values_ready"))
        silu_ready = sem("silu_ready")
        ws_in, tables_in, ws_turned, ws_masked = sem("ws_in"), sem("tables_in"), sem("ws_turned"), sem("ws_masked")
        var_ready, sgu_root, sgu_normed, mixed_ready = (sem("var_ready"), sem("sgu_root"), sem("sgu_normed"),
                                                        sem("mixed_ready"))
        conv_done, sgu_done = sem("conv_done"), sem("sgu_done")
        y_heads, y_tails, m_heads, m_tails = sem("y_heads"), sem("y_tails"), sem("m_heads"), sem("m_tails")
        h_back, ln1_in, summed_out = sem("h_back"), sem("ln1_in"), sem("summed_out")
        var1_ready, root1_done = sem("var1_ready"), sem("root1_done")
        dense_order = sem("dense_order")
        router_in, r_turned, r_copied, logits_ready = (sem("router_in"), sem("r_turned"), sem("r_copied"),
                                                       sem("logits_ready"))
        r_shift, r_exp, chosen, counted, slots_ready, scattered = (
            sem("r_shift"), sem("r_exp"), sem("chosen"), sem("counted"), sem("slots_ready"), sem("scattered"))
        route_order = sem("route_order")
        e_raw_in = [sem(f"e_raw_in{i}") for i in range(NER)]
        e_heads, e_tails, e_used = sem("e_heads"), sem("e_tails"), sem("e_used")
        x_in, e_turned, e_t_heads, e_t_tails = sem("x_in"), sem("e_turned"), sem("e_t_heads"), sem("e_t_tails")
        sig_done, gated, out_moved, y_stored = sem("sig_done"), sem("gated"), sem("out_moved"), sem("y_stored")
        out_free = sem("out_free")
        e_order = sem("e_order")
        gathered, ln2_in, c_order, var2_ready, root2_done, h_final, h_stored = (
            sem("gathered"), sem("ln2_in"), sem("c_order"), sem("var2_ready"), sem("root2_done"), sem("h_final"),
            sem("h_stored"))

        for s in setup_sems:
            nc.gpsimd.sem_clear(s)
        nc.all_engine_barrier()

        free_by, n_z, n_gate, n_merge, n_out = [], 0, 0, 0, 0
        for x in plan:
            if x["kind"] == "ZT":
                n_z += 1
                free_by.append((z_moved, n_z))
            elif x["kind"] == "ZN":
                n_z += x["half"]
                free_by.append((z_moved, n_z + 1 - x["half"]))
            elif x["kind"] == "gate":
                n_gate += 1
                free_by.append((gates_done, n_gate))
            elif x["kind"] == "branch":
                n_merge += 1
                free_by.append((merged_done, n_merge))
            else:
                n_out += x["half"]
                free_by.append((summed_out, n_out + 1 - x["half"]))
        z_count = {}
        n = 0
        for x in plan:
            if x["kind"] == "ZT" or (x["kind"] == "ZN" and x["half"]):
                n += 1
                z_count[(x["b"], x["g"], x["half"])] = n
        z_all = {b: max(v for k, v in z_count.items() if k[0] == b) for b in ORDER}
        gate_chunk = {b: [c for c, x in enumerate(plan) if x["kind"] == "gate" and x["b"] == b] for b in ORDER}
        y_of = {CONV: z1[:, 2], DIFF: z0[:, 0], RET: z1[:, 2], SGU: z0[:, 0]}
        y_done = {CONV: (conv_done, 4), DIFF: (normed, 4), RET: (normed, 8), SGU: (sgu_done, 1)}
        turned_before_norm = {hd: min(4 * TT, (hd + 1) * TT + 2) for hd in range(4)}

        def is_narrow(x):
            return x["kind"] in ("ZT", "gate", "branch")

        def raw_view(buf, x):
            if x["kind"] == "branch":
                return buf[:, 0:1024].rearrange("p (k n) -> p k n", k=4)
            if is_narrow(x):
                return buf[:, :].rearrange("p (k n) -> p k n", k=8)
            return buf[:, :].rearrange("p (k n) -> p k n", k=4)

        with nc.Fori(0, DEPTH) as layer:
            with nc.Block() as block:
                @block.sync
                def _(sp):
                    def source(x):
                        if x["kind"] == "ZT":
                            c0 = x["tile"] * W + x["half"] * 256
                            return a["w_in"][layer].rearrange("(k p) n -> p k n", p=P)[:, :, c0:c0 + 256]
                        if x["kind"] == "ZN":
                            return a["w_in"][layer].rearrange("(k p) n -> p k n", p=P)[
                                :, 4 * x["half"]:4 * x["half"] + 4, x["tile"] * W:(x["tile"] + 1) * W]
                        if x["kind"] == "gate":
                            return a["w_gate"][layer, x["b"]].rearrange("(k p) n -> p k n", p=P)[
                                :, :, x["q"] * 256:x["q"] * 256 + 256]
                        if x["kind"] == "branch":
                            return a["w_branch"][layer, x["b"]].rearrange("(k p) n -> p k n", p=P)[
                                :, :, x["q"] * 256:x["q"] * 256 + 256]
                        return a["w_o"][layer].rearrange("(k p) n -> p k n", p=P)[
                            :, 4 * x["half"]:4 * x["half"] + 4, x["n"] * 512:x["n"] * 512 + 512]

                    for c, x in enumerate(plan):
                        if c >= NRAW:
                            sp.wait_ge(tails, c - NRAW + 1)
                        sp.dma_start(raw_view(raw[c % NRAW], x), source(x)).then_inc(raw_in[c % NRAW], 16)

                @block.gpsimd
                def _(pool):
                    pool.dma_start(prow[0:32, :], a["b_gate"][layer].rearrange("b (m p) -> (b m) p", p=P))\
                        .then_inc(params_in, 16)
                    pool.dma_start(prow[32:44, :], a["conv_w"][layer].rearrange("k o (m p) -> (k o m) p", p=P))\
                        .then_inc(params_in, 16)
                    pool.dma_start(prow[44:45, :], a["diff_subln_g"][bass.ds(layer, 1), :]).then_inc(params_in, 16)
                    for i, name in enumerate(("lambda_q1", "lambda_q2", "lambda_k1", "lambda_k2")):
                        pool.dma_start(lam_rows[:, i, :], a[name][bass.ds(layer, 1), :].to_broadcast((P, 64)))\
                            .then_inc(params_in, 16)
                    lo = CONST["lam"][0]
                    pool.dma_start(lam_in, a["consts"][:, bass.ds(layer * 2 + lo, 2)]).then_inc(params_in, 16)
                    for hd in range(4):
                        if hd >= 2:
                            pool.wait_ge(decayed, hd - 1)
                        pool.dma_start(decay[:, hd % 2, :], a["decay"][hd]).then_inc(decay_in[hd % 2], 16)
                        if hd == 1:
                            pool.wait_ge(att_turned, 4 * TT)
                            pool.dma_start(att[:, 0, :].rearrange("p (g s) -> p g s", g=4),
                                           a["w_s"][layer].rearrange("g t s -> t g s")).then_inc(ws_in, 16)
                    pool.wait_ge(decayed, 4)
                    pool.dma_start(decay[:, 0, :], a["sgu_ln_g"][bass.ds(layer, 1), :].to_broadcast((P, W)))\
                        .then_inc(tables_in, 16)
                    pool.dma_start(decay[:, 1, :], a["sgu_ln_b"][bass.ds(layer, 1), :].to_broadcast((P, W)))\
                        .then_inc(tables_in, 16)
                    pool.wait_ge(ret_values_ready, 4)
                    pool.dma_start(attT[:, 0, :], a["b_s"][bass.ds(layer, 1)].rearrange("a g t -> a (g t)")
                                   .to_broadcast((P, W))).then_inc(tables_in, 16)
                    pool.wait_ge(y_tails, 3)
                    pool.dma_start(ln1_gb[:, 0, :], a["ln1_g"][bass.ds(layer, 1), :].to_broadcast((P, D)))\
                        .then_inc(ln1_in, 16)
                    pool.dma_start(ln1_gb[:, 1, :], a["ln1_b"][bass.ds(layer, 1), :].to_broadcast((P, D)))\
                        .then_inc(ln1_in, 16)
                    pool.wait_ge(y_tails, 4)
                    pool.dma_start(h[:], out[0].rearrange("(t p) d -> p t d", p=P)).then_inc(h_back, 16)
                    for s, n in ((params_in, 128), (decay_in[0], 32), (decay_in[1], 32), (ws_in, 16), (tables_in, 48),
                                 (ln1_in, 32), (h_back, 16)):
                        pool.wait_ge(s, n)

                @block.scalar
                def _(act):
                    def head(c):
                        x = plan[c]
                        act.wait_ge(raw_in[c % NRAW], 16 * (c // NRAW + 1))
                        if c >= 2:
                            act.wait_ge(chunk_used, c - 1)
                        act.activation(raw_view(w_head[c % 2], x), raw_view(raw[c % NRAW], x), ACT.Copy)\
                           .then_inc(heads, 1)

                    def unit(kind, *g):
                        if kind == "split":
                            b = g[0]
                            i = ORDER.index(b)
                            act.wait_ge(*y_done[b])
                            if i:
                                act.wait_ge(chunk_used, gate_chunk[ORDER[i - 1]][-1] + 2)
                            act.activation(yT_head[:], y_of[b], ACT.Copy).then_inc(y_heads, 1)
                        elif kind == "diff_scores":
                            u, w = g[0], P * (g[0] % TT + 1)
                            act.wait_ge(masked, u + 1)
                            for c in range(2):
                                i = act.activation(att[:, c, 0:w], att[:, c, 0:w], ACT.Exp, bias=top[:, c:c + 1],
                                                   scale=0.125, accum_out=rowsum[:, c:c + 1])
                            i.then_inc(exps_done, 1)
                        elif kind == "diff_transpose":
                            u, it = g[0], g[0] % TT
                            act.wait_ge(att_turned, u + 1)
                            if u >= TT:
                                act.wait_ge(values_ready, u // TT)
                            act.activation(attT[:, 0:it + 1, it * P:(it + 1) * P],
                                           ps[:, 6, 0:(it + 1) * P].rearrange("p (j i) -> p j i", i=P), ACT.Copy)\
                               .then_inc(att_copied, 1)
                        elif kind in ("diff_values", "ret_values"):
                            n = g[0] + (4 if kind == "ret_values" else 0)
                            act.wait_ge(ret_values_ready if n >= 4 else values_ready, g[0] + 1)
                            if n:
                                act.wait_ge(summed, n)
                            act.activation(square[:], ps[:, 4 if n >= 4 else 7, :], ACT.Square).then_inc(squared, 1)
                            if n >= 4:
                                act.wait_ge(normed, n)
                                act.activation(silu[:], z1[:, 2, g[0], :], ACT.Sigmoid).then_inc(silu_ready, 1)
                        elif kind in ("diff_norm", "ret_norm"):
                            n = g[0] + (4 if kind == "ret_norm" else 0)
                            act.wait_ge(summed, n + 1)
                            if n:
                                act.wait_ge(normed, n)
                            act.activation(std[:], ps[:, 5 if n >= 4 else 6, :], ACT.Sqrt, scale=1.0 / 128,
                                           bias=const("eps")[:, 1:2]).then_inc(rooted, 1)
                        elif kind == "sgu_norm":
                            n = g[0]
                            act.wait_ge(var_ready, n + 1)
                            act.activation(ln_sd[:, n:n + 1], ln_mv[:, n, 1:2], ACT.Sqrt, bias=const("eps")[:, 0:1])\
                               .then_inc(sgu_root, 1)
                        elif kind == "merge_split":
                            q = g[0]
                            act.wait_ge(chunk_used, gate_chunk[SGU][-1] + 1)
                            act.wait_ge(merged_done, 4 * 3 + q + 1)
                            act.activation(hT_head[:, 2 * q:2 * q + 2, :], merged[:, 2 * q:2 * q + 2, :], ACT.Copy)\
                               .then_inc(m_heads, 1)

                    head(0)
                    head(1)
                    for k in range(KD):
                        act.wait_ge(h_turned, k + 1)
                        act.activation(hT_head[:, k, :], ps[:, k, :], ACT.Copy).then_inc(hT_heads, 1)
                    act.wait_ge(lam_exp_in, 1)
                    act.activation(lam[:, 0:2], lam[:, 2:4], ACT.Exp).then_inc(lam_exp, 1)
                    for c, x in enumerate(plan):
                        for unit_ in x["mid"]:
                            unit(*unit_)
                        banks = slice(2 * (c % 2), 2 * (c % 2) + 2)
                        if x["kind"] in ("ZT", "ZN") and not (x["kind"] == "ZN" and not x["half"]):
                            act.wait_ge(chunk_used, c + 1)
                            if x["b"] == RET:
                                act.wait_ge(y_tails, 1)
                            if x["b"] == SGU:
                                act.wait_ge(y_tails, 2)
                            if x["kind"] == "ZT":
                                act.activation(z[ZBUF[x["b"]]][:, x["g"], 2 * x["half"]:2 * x["half"] + 2, :],
                                               ps[:, banks, :], ACT.Copy).then_inc(z_moved, 1)
                            else:
                                act.activation(z[ZBUF[x["b"]]][:, x["g"], :, :], ps[:, 0:4, :], ACT.Copy)\
                                   .then_inc(z_moved, 1)
                        if x["kind"] == "gate":
                            n = free_by[c][1]
                            act.wait_ge(chunk_used, c + 1)
                            if n > 1:
                                act.wait_ge(merged_done, n - 1)
                            else:
                                act.wait_ge(prm_ready, 1)
                            for m in range(2):
                                bias = prm[:, x["b"] * 8 + 2 * x["q"] + m:x["b"] * 8 + 2 * x["q"] + m + 1]
                                i = act.activation(gate[:, m, :], ps[:, 2 * (c % 2) + m, :], ACT.Sigmoid, bias=bias)
                            i.then_inc(gates_done, 1)
                        if c + 2 < nchunk:
                            head(c + 2)
                        for unit_ in x["units"]:
                            unit(*unit_)
                    act.wait_ge(var1_ready, 1)
                    act.activation(ln_sd, ln_mv[:, :, 1], ACT.Sqrt, bias=const("eps")[:, 0:1]).then_inc(root1_done, 1)

                @block.vector
                def _(v):
                    order = Steps(v, dense_order)

                    def tail(c):
                        x = plan[c]
                        v.wait_ge(heads, c + 1)
                        v.tensor_tensor(raw_view(w_tail[c % 2], x), raw_view(raw[c % NRAW], x),
                                        raw_view(w_head[c % 2], x), ALU.subtract).then_inc(tails, 1)

                    def unit(kind, *g):
                        if kind == "split":
                            v.wait_ge(y_heads, ORDER.index(g[0]) + 1)
                            v.tensor_tensor(yT_tail[:], y_of[g[0]], yT_head[:], ALU.subtract).then_inc(y_tails, 1)
                        elif kind == "conv":
                            m = g[0]
                            if m == 0:
                                v.wait_ge(z_moved, z_all[CONV])
                            bg, cg, ug = z1[:, 0, m, :], z1[:, 1, m, :], z1[:, 2, m, :]

                            def tap(k):
                                return prm[:, 32 + 4 * k + m:33 + 4 * k + m]

                            order.then(v.tensor_tensor(cg, cg, ug, ALU.mult))
                            order.then(v.tensor_scalar(ug, cg, tap(2), None, ALU.mult))
                            for s in (1, 2):
                                order.then(v.scalar_tensor_tensor(out=ug[:, s:T], in0=cg[:, 0:T - s], scalar=tap(2 - s),
                                                                  in1=ug[:, s:T], op0=ALU.mult, op1=ALU.add))
                            v.tensor_tensor(ug, ug, bg, ALU.mult).then_inc(conv_done, 1)
                        elif kind == "rotate":
                            b, grp = g
                            n = 3 if b == RET else grp + 1
                            co, si = (cos_ret, sin_ret) if b == RET else (cos_diff, sin_diff)
                            x = z[ZBUF[b]][:, grp]
                            cob, sib = (s[:, :].unsqueeze(1).to_broadcast((P, 4, T)) for s in (co, si))
                            v.wait_ge(swapped, n)
                            order.then(v.tensor_tensor(x, x, cob, ALU.mult))
                            order.then(v.tensor_tensor(attT[:], ps[:, 4:8, :], sib, ALU.mult))
                            v.tensor_tensor(x, x, attT[:], ALU.add).then_inc(rotated, 1)
                            v.wait_ge(rotated, n)
                        elif kind == "diff_scores":
                            u, it = g[0], g[0] % TT
                            w = P * (it + 1)
                            v.wait_ge(scores_ready, u + 1)
                            if u:
                                v.wait_ge(att_turned, u)
                            m = causal[:, T - w:T].unsqueeze(1).to_broadcast((P, 2, w))
                            order.then(v.tensor_tensor(att[:, :, 0:w], ps[:, 4:6, 0:w], m, ALU.add))
                            order.then(v.tensor_reduce(top, att[:, :, 0:w], AX, ALU.max))
                            v.tensor_scalar(top, top, -0.125, None, ALU.mult).then_inc(masked, 1)
                            v.wait_ge(exps_done, u + 1)
                            order.then(v.reciprocal(rowsum, rowsum))
                            order.then(v.tensor_tensor(rowsum[:, 1:2], rowsum[:, 1:2], lam[:, 2:3], ALU.mult))
                            order.then(v.tensor_scalar(att[:, 0, 0:w], att[:, 0, 0:w], rowsum[:, 0:1], None, ALU.mult))
                            v.scalar_tensor_tensor(out=att[:, 0, 0:w], in0=att[:, 1, 0:w], scalar=rowsum[:, 1:2],
                                                   in1=att[:, 0, 0:w], op0=ALU.mult, op1=ALU.add).then_inc(att_ready, 1)
                        elif kind == "diff_norm":
                            hd = g[0]
                            v.wait_ge(rooted, hd + 1)
                            order.then(v.reciprocal(std[:], std[:]))
                            v.scalar_tensor_tensor(out=z0[:, 0, hd, :], in0=ps[:, 7, :], scalar=lam[:, 3:4], in1=std[:],
                                                   op0=ALU.mult, op1=ALU.mult).then_inc(normed, 1)
                        elif kind == "ret_scores":
                            hd = g[0]
                            v.wait_ge(ret_scores_ready, hd + 1)
                            v.wait_ge(decay_in[hd % 2], 16 * (hd // 2 + 1))
                            if hd:
                                v.wait_ge(ret_values_ready, hd)
                            for jt in range(TT):
                                w = T - jt * P
                                i = v.tensor_tensor(attT[:, jt, 0:w], ps[:, 4 + jt, 0:w], decay[:, hd % 2, 0:w], ALU.mult)
                            i.then_inc(decayed, 1)
                        elif kind == "ret_norm":
                            hd = g[0]
                            v.wait_ge(silu_ready, hd + 1)
                            order.then(v.tensor_tensor(silu[:], silu[:], z1[:, 2, hd, :], ALU.mult))
                            v.wait_ge(rooted, 4 + hd + 1)
                            order.then(v.reciprocal(std[:], std[:]))
                            order.then(v.tensor_tensor(silu[:], silu[:], std[:], ALU.mult))
                            v.tensor_tensor(z1[:, 2, hd, :], ps[:, 4, :], silu[:], ALU.mult).then_inc(normed, 1)
                        elif kind == "sgu_mask":
                            v.wait_ge(ws_turned, 1)
                            v.tensor_tensor(att[:, 1, :].rearrange("p (g s) -> p g s", g=4),
                                            ps[:, 4, :].rearrange("p (g s) -> p g s", g=4),
                                            const("upper").unsqueeze(1).to_broadcast((P, 4, P)), ALU.mult)\
                             .then_inc(ws_masked, 1)
                        elif kind == "sgu_norm":
                            n = g[0]
                            x = z0[:, 1, n, :]
                            if n == 0:
                                v.wait_ge(z_moved, z_all[SGU])
                                v.wait_ge(tables_in, 48)
                            order.then(v.bn_stats(ln_stats[:, n, 0, :], x))
                            v.bn_aggr(ln_mv[:, n, :], ln_stats[:, n, 0, :]).then_inc(var_ready, 1)
                            v.wait_ge(sgu_root, n + 1)
                            order.then(v.reciprocal(ln_sd[:, n:n + 1], ln_sd[:, n:n + 1]))
                            order.then(v.tensor_scalar(x, x, ln_mv[:, n, 0:1], ln_sd[:, n:n + 1], ALU.subtract, ALU.mult))
                            order.then(v.tensor_tensor(x, x, decay[:, 0, :], ALU.mult))
                            v.tensor_tensor(x, x, decay[:, 1, :], ALU.add).then_inc(sgu_normed, 1)
                        elif kind == "sgu_mix":
                            v.wait_ge(mixed_ready, 1)
                            s4 = z0[:, 1].rearrange("p g (n t) -> p g n t", t=P)
                            for grp in range(4):
                                i = v.tensor_tensor(s4[:, grp], ps[:, 4 + grp, :].rearrange("p (n t) -> p n t", t=P),
                                                    attT[:, 0, grp * P:(grp + 1) * P].unsqueeze(1).to_broadcast((P, 4, P)),
                                                    ALU.add)
                            order.then(i)
                            v.tensor_tensor(z0[:, 0], z0[:, 0], z0[:, 1], ALU.mult).then_inc(sgu_done, 1)
                        elif kind == "merge_split":
                            q = g[0]
                            v.wait_ge(m_heads, q + 1)
                            v.tensor_tensor(hT_tail[:, 2 * q:2 * q + 2, :], merged[:, 2 * q:2 * q + 2, :],
                                            hT_head[:, 2 * q:2 * q + 2, :], ALU.subtract).then_inc(m_tails, 1)

                    tail(0)
                    tail(1)
                    for k in range(KD):
                        v.wait_ge(hT_heads, k + 1)
                        v.tensor_tensor(hT_tail[:, k, :], ps[:, k, :], hT_head[:, k, :], ALU.subtract).then_inc(hT_tails, 1)
                    v.wait_ge(prm_turned, 1)
                    v.tensor_copy(prm[:], ps[:, 4, 0:45]).then_inc(prm_ready, 1)
                    v.wait_ge(prm_ready, 1)
                    order.then(v.tensor_tensor(lam_rows[:, 0:2, :], lam_rows[:, 0:2, :], lam_rows[:, 2:4, :], ALU.mult))
                    v.tensor_reduce(lam[:, 2:4], lam_rows[:, 0:2, :], AX, ALU.add).then_inc(lam_exp_in, 1)
                    v.wait_ge(lam_exp, 1)
                    order.then(v.tensor_tensor(lam[:, 2:3], lam[:, 1:2], lam[:, 0:1], ALU.subtract))
                    order.then(v.tensor_tensor(lam[:, 2:3], lam[:, 2:3], lam_in[:, 0:1], ALU.subtract))
                    order.then(v.tensor_tensor(lam[:, 3:4], prm[:, 44:45], lam_in[:, 1:2], ALU.mult))
                    for c, x in enumerate(plan):
                        for unit_ in x["mid"]:
                            unit(*unit_)
                        if x["kind"] == "branch":
                            n = free_by[c][1]
                            q = x["q"]
                            bank = 2 * (c % 2)
                            v.wait_ge(chunk_used, c + 1)
                            v.wait_ge(gates_done, n)
                            m2 = merged[:, 2 * q:2 * q + 2, :]
                            if x["b"] == ORDER[0]:
                                v.tensor_tensor(m2, ps[:, bank:bank + 2, :], gate[:], ALU.mult).then_inc(merged_done, 1)
                            else:
                                order.then(v.tensor_tensor(gate[:], ps[:, bank:bank + 2, :], gate[:], ALU.mult))
                                v.tensor_tensor(m2, m2, gate[:], ALU.add).then_inc(merged_done, 1)
                        if x["kind"] == "wo" and x["half"]:
                            v.wait_ge(chunk_used, c + 1)
                            v.wait_ge(h_back, 16)
                            hn = h[:, :, x["n"] * 512:x["n"] * 512 + 512]
                            v.scalar_tensor_tensor(out=hn, in0=hn, scalar=ALPHA, in1=ps[:, 0:4, :], op0=ALU.mult,
                                                   op1=ALU.add).then_inc(summed_out, 1)
                        if c + 2 < nchunk:
                            tail(c + 2)
                        for unit_ in x["units"]:
                            unit(*unit_)
                    v.wait_ge(summed_out, 2)
                    for t in range(TT):
                        layer_norm_stats(v, order, h[:, t, :], 2, ln_stats[:, t], ln_mv[:, t, :])
                    v.engine_nop().then_inc(var1_ready, 1)
                    v.wait_ge(root1_done, 1)
                    v.wait_ge(ln1_in, 32)
                    order.then(v.reciprocal(ln_sd, ln_sd))
                    for t in range(TT):
                        order.then(v.tensor_scalar(h[:, t, :], h[:, t, :], ln_mv[:, t, 0:1], ln_sd[:, t:t + 1],
                                                   ALU.subtract, ALU.mult))
                    order.then(v.tensor_tensor(h[:], h[:], ln1_gb[:, 0:1, :].to_broadcast((P, TT, D)), ALU.mult))
                    order.then(v.tensor_tensor(h[:], h[:], ln1_gb[:, 1:2, :].to_broadcast((P, TT, D)), ALU.add))

                @block.tensor
                def _(pe):
                    ident = const("ident")

                    def products(c, x, half):
                        wh, wt = raw_view(w_head[c % 2], x), raw_view(w_tail[c % 2], x)
                        if is_narrow(x):
                            nk, (xh, xt) = (4, (yT_head, yT_tail)) if x["kind"] == "branch" else (8, (hT_head, hT_tail))
                            m = half
                            o = ps[:, 2 * (c % 2) + m, :]
                            for k in range(nk):
                                lh, lt = wh[:, k, m * P:(m + 1) * P], wt[:, k, m * P:(m + 1) * P]
                                nc.tensor.matmul(o, lh, xh[:, k, :], start=k == 0, stop=False)
                                nc.tensor.matmul(o, lh, xt[:, k, :], start=False, stop=False)
                                i = nc.tensor.matmul(o, lt, xh[:, k, :], start=False, stop=k == nk - 1)
                        else:
                            k0 = 4 * x["half"]
                            for m in (2 * half, 2 * half + 1):
                                o = ps[:, m, :]
                                for k in range(4):
                                    lh = hT_head[:, k0 + k, m * P:(m + 1) * P]
                                    lt = hT_tail[:, k0 + k, m * P:(m + 1) * P]
                                    nc.tensor.matmul(o, lh, wh[:, k, :], start=x["half"] == 0 and k == 0, stop=False)
                                    nc.tensor.matmul(o, lh, wt[:, k, :], start=False, stop=False)
                                    i = nc.tensor.matmul(o, lt, wh[:, k, :], start=False,
                                                         stop=x["half"] == 1 and k == 3)
                        return i

                    def unit(kind, *g):
                        if kind == "rotate":
                            b, grp = g
                            n = 3 if b == RET else grp + 1
                            if b == RET:
                                pe.wait_ge(z_moved, z_count[(RET, 0, 1)])
                                pe.wait_ge(normed, 4)
                                pe.wait_ge(att_copied, 4 * TT)
                            else:
                                pe.wait_ge(z_moved, z_count[(DIFF, grp, 1)])
                                if n > 1:
                                    pe.wait_ge(rotated, n - 1)
                                else:
                                    pe.wait_ge(prm_ready, 1)
                            for m in range(4):
                                i = nc.tensor.matmul(ps[:, 4 + m, :], const("swap_ret" if b == RET else "swap_diff"),
                                                     z[ZBUF[b]][:, grp, m, :], start=True, stop=True)
                            i.then_inc(swapped, 1)
                        elif kind == "diff_scores":
                            u, hd, it = g[0], g[0] // TT, g[0] % TT
                            w = P * (it + 1)
                            if u:
                                pe.wait_ge(masked, u)
                            else:
                                pe.wait_ge(rotated, 2)
                            for c in range(2):
                                rows = slice(64 * c, 64 * c + 64)
                                i = nc.tensor.matmul(ps[:, 4 + c, 0:w], z0[rows, 0, hd, it * P:(it + 1) * P],
                                                     z0[rows, 1, hd, 0:w], start=True, stop=True)
                            i.then_inc(scores_ready, 1)
                        elif kind == "diff_transpose":
                            u, it = g[0], g[0] % TT
                            pe.wait_ge(att_ready, u + 1)
                            if u:
                                pe.wait_ge(att_copied, u)
                            done = [hd for hd in range(4) if turned_before_norm[hd] <= u]
                            if done:
                                pe.wait_ge(rooted, len(done))
                            for j in range(it + 1):
                                i = nc.tensor.transpose(ps[:, 6, j * P:(j + 1) * P], att[:, 0, j * P:(j + 1) * P], ident)
                            i.then_inc(att_turned, 1)
                        elif kind == "diff_values":
                            hd = g[0]
                            pe.wait_ge(att_copied, TT * (hd + 1))
                            if hd == 0:
                                pe.wait_ge(z_moved, z_all[DIFF])
                            else:
                                pe.wait_ge(normed, hd)
                            for j in range(TT):
                                i = nc.tensor.matmul(ps[:, 7, j * P:T], z0[:, 2, j, hd * P:(hd + 1) * P],
                                                     attT[:, j, j * P:T], start=j == 0, stop=j == TT - 1)
                            i.then_inc(values_ready, 1)
                        elif kind == "diff_norm":
                            hd = g[0]
                            pe.wait_ge(squared, hd + 1)
                            pe.wait_ge(att_copied, turned_before_norm[hd])
                            nc.tensor.matmul(ps[:, 6, :], const("ones"), square[:], start=True, stop=True)\
                              .then_inc(summed, 1)
                        elif kind == "ret_scores":
                            hd = g[0]
                            r, m = slice(64 * (hd % 2), 64 * (hd % 2) + 64), hd // 2
                            if hd == 0:
                                pe.wait_ge(rotated, 3)
                            else:
                                pe.wait_ge(normed, 4 + hd)
                            for j in range(TT):
                                i = nc.tensor.matmul(ps[:, 4 + j, 0:T - j * P], z1[r, 0, 2 + m, j * P:(j + 1) * P],
                                                     z1[r, 0, m, j * P:T], start=True, stop=True)
                            i.then_inc(ret_scores_ready, 1)
                        elif kind == "ret_values":
                            hd = g[0]
                            if hd == 0:
                                pe.wait_ge(z_moved, z_all[RET])
                            pe.wait_ge(decayed, hd + 1)
                            for j in range(TT):
                                i = nc.tensor.matmul(ps[:, 4, j * P:T], z1[:, 1, j, hd * P:(hd + 1) * P],
                                                     attT[:, j, 0:T - j * P], start=j == 0, stop=j == TT - 1)
                            i.then_inc(ret_values_ready, 1)
                        elif kind == "ret_norm":
                            pe.wait_ge(squared, 4 + g[0] + 1)
                            nc.tensor.matmul(ps[:, 5, :], const("ones"), square[:], start=True, stop=True)\
                              .then_inc(summed, 1)
                        elif kind == "sgu_mask":
                            pe.wait_ge(ws_in, 16)
                            pe.wait_ge(normed, 8)
                            for grp in range(4):
                                i = nc.tensor.transpose(ps[:, 4, grp * P:(grp + 1) * P], att[:, 0, grp * P:(grp + 1) * P],
                                                        ident)
                            i.then_inc(ws_turned, 1)
                        elif kind == "sgu_mix":
                            pe.wait_ge(ws_masked, 1)
                            pe.wait_ge(sgu_normed, TT)
                            for grp in range(4):
                                for n in range(TT):
                                    i = nc.tensor.matmul(ps[:, 4 + grp, n * P:(n + 1) * P],
                                                         z0[:, 1, n, grp * P:(grp + 1) * P],
                                                         att[:, 1, grp * P:(grp + 1) * P], start=True, stop=True)
                            i.then_inc(mixed_ready, 1)

                    for k in range(KD):
                        for t in range(TT):
                            i = nc.tensor.transpose(ps[:, k, t * P:(t + 1) * P], h[:, t, k * P:(k + 1) * P], ident)
                        i.then_inc(h_turned, 1)
                    pe.wait_ge(params_in, 128)
                    pe.wait_ge(hT_tails, KD)
                    nc.tensor.transpose(ps[:, 4, 0:45], prow[:], ident[0:45, 0:45]).then_inc(prm_turned, 1)
                    for c, x in enumerate(plan):
                        pe.wait_ge(tails, c + 1)
                        if c >= 2:
                            pe.wait_ge(*free_by[c - 2])
                        if c >= 1 and not is_narrow(x):
                            pe.wait_ge(*free_by[c - 1]) if free_by[c - 1] != free_by[c] else None
                        if x["kind"] == "branch":
                            pe.wait_ge(y_tails, ORDER.index(x["b"]) + 1)
                        if x["kind"] == "wo":
                            pe.wait_ge(m_tails, 2 * x["half"] + 2)
                        products(c, x, 0)
                        for unit_ in x["mid"]:
                            unit(*unit_)
                        products(c, x, 1).then_inc(chunk_used, 1)
                        for unit_ in x["units"]:
                            unit(*unit_)

            with nc.Block() as block:
                def r(i):
                    return route[:, i, :].rearrange("p (t e) -> p t e", e=E)

                def over_e(x):
                    return x.unsqueeze(2).to_broadcast((P, TT, E))

                def over_t(x, n=E):
                    return x.unsqueeze(1).to_broadcast((P, TT, n))

                LOGIT, SCORE, SEL, MASKED, WEIGHT, ONE, TWO, BOTH, RANK, DEST, TMP = range(11)

                @block.sync
                def _(sp):
                    sp.dma_start(w_router[:], a["w_router"].rearrange("(k p) e -> p k e", p=P)).then_inc(router_in, 16)
                    sp.dma_start(b_router[:], a["b_router"].rearrange("(a e) -> a e", a=1).to_broadcast((P, E)))\
                      .then_inc(router_in, 16)

                @block.gpsimd
                def _(pool):
                    pool.wait_ge(slots_ready, 1)
                    for i in range(2):
                        for t in range(TT):
                            pool.indirect_dma_start(slot_x[:, :], bass.IndirectOffsetOnAxis(slots[:, i, t:t + 1], 0),
                                                    h[:, t, :], None).then_inc(scattered, 16)
                    pool.wait_ge(scattered, 16 * 2 * TT)

                @block.scalar
                def _(act):
                    for k in range(0, KD, 2):
                        act.wait_ge(r_turned, k + 2)
                        act.activation(hT[:, k:k + 2, :], ps[:, k:k + 2, :], ACT.Copy).then_inc(r_copied, 1)
                    act.wait_ge(r_shift, 1)
                    act.activation(r(SCORE), r(LOGIT), ACT.Exp).then_inc(r_exp, 1)

                @block.tensor
                def _(pe):
                    for k in range(KD):
                        for t in range(TT):
                            i = nc.tensor.transpose(ps[:, k, t * P:(t + 1) * P], h[:, t, k * P:(k + 1) * P],
                                                    const("ident"))
                        i.then_inc(r_turned, 1)
                    pe.wait_ge(router_in, 32)
                    pe.wait_ge(r_copied, KD // 2)
                    for t in range(TT):
                        for k in range(KD):
                            i = nc.tensor.matmul(ps[:, 0, t * E:(t + 1) * E], hT[:, k, t * P:(t + 1) * P],
                                                 w_router[:, k, :], start=k == 0, stop=k == KD - 1)
                    i.then_inc(logits_ready, 1)
                    pe.wait_ge(chosen, 1)
                    for t in range(TT):
                        for s in range(t + 1):
                            nc.tensor.matmul(ps[:, 1, t * E:(t + 1) * E], const("strict" if s == t else "ones"),
                                             r(BOTH)[:, s, :], start=s == 0, stop=s == t)
                    for s in range(TT):
                        i = nc.tensor.matmul(ps[:, 2, 0:E], const("ones"), r(BOTH)[:, s, :], start=s == 0,
                                             stop=s == TT - 1)
                    i.then_inc(counted, 1)

                @block.vector
                def _(v):
                    order = Steps(v, route_order)
                    pairs = [route[:, 12 + i, 0:TT * NG] for i in range(8)]
                    row = [route[:, 20 + i, 0:TT] for i in range(4)]

                    def first_max(src, onehot, by, n, top_, weights):
                        b3 = (P, TT, n)
                        order.then(v.tensor_reduce(top_, src, AX, ALU.max))
                        order.then(v.tensor_tensor(weights, src, top_.unsqueeze(2).to_broadcast(b3), ALU.is_equal))
                        order.then(v.tensor_tensor(weights, weights, over_t(by, n), ALU.mult))
                        order.then(v.tensor_reduce(top_, weights, AX, ALU.max))
                        order.then(v.tensor_tensor(onehot, weights, top_.unsqueeze(2).to_broadcast(b3), ALU.is_equal))

                    v.wait_ge(logits_ready, 1)
                    order.then(v.tensor_copy(r(LOGIT), ps[:, 0, 0:TT * E].rearrange("p (t e) -> p t e", e=E)))
                    order.then(v.tensor_reduce(row[0], r(LOGIT), AX, ALU.max))
                    v.tensor_tensor(r(LOGIT), r(LOGIT), over_e(row[0]), ALU.subtract).then_inc(r_shift, 1)
                    v.wait_ge(r_exp, 1)
                    order.then(v.tensor_reduce(row[0], r(SCORE), AX, ALU.add))
                    order.then(v.reciprocal(row[0], row[0]))
                    order.then(v.tensor_tensor(r(SCORE), r(SCORE), over_e(row[0]), ALU.mult))
                    order.then(v.tensor_tensor(r(SEL), r(SCORE), over_t(b_router[:, :]), ALU.add))
                    s4 = route[:, SEL, :].rearrange("p (g e) -> p g e", e=EG)
                    hi1, lo1, hi2, lo2, t1, t2 = pairs[:6]
                    order.then(v.tensor_tensor(hi1, s4[:, :, 0], s4[:, :, 1], ALU.max))
                    order.then(v.tensor_tensor(lo1, s4[:, :, 0], s4[:, :, 1], ALU.min))
                    order.then(v.tensor_tensor(hi2, s4[:, :, 2], s4[:, :, 3], ALU.max))
                    order.then(v.tensor_tensor(lo2, s4[:, :, 2], s4[:, :, 3], ALU.min))
                    order.then(v.tensor_tensor(t1, hi1, hi2, ALU.max))
                    order.then(v.tensor_tensor(t2, hi1, hi2, ALU.min))
                    order.then(v.tensor_tensor(lo1, lo1, lo2, ALU.max))
                    order.then(v.tensor_tensor(t2, t2, lo1, ALU.max))
                    order.then(v.tensor_tensor(t1, t1, t2, ALU.add))
                    g3 = t1.rearrange("p (t g) -> p t g", g=NG)
                    best = t2.rearrange("p (t g) -> p t g", g=NG)
                    first_max(g3, best, const("first_g"), NG, row[1], hi1.rearrange("p (t g) -> p t g", g=NG))
                    m4 = route[:, MASKED, :].rearrange("p (g e) -> p g e", e=EG)
                    order.then(v.tensor_scalar(t2, t2, -NEG, NEG, ALU.mult, ALU.add))
                    order.then(v.tensor_tensor(m4, s4, t2.unsqueeze(2).to_broadcast((P, TT * NG, EG)), ALU.add))
                    first_max(r(MASKED), r(ONE), const("first_e"), E, row[1], r(WEIGHT))
                    order.then(v.scalar_tensor_tensor(out=r(MASKED), in0=r(ONE), scalar=3 * NEG, in1=r(MASKED),
                                                      op0=ALU.mult, op1=ALU.add))
                    first_max(r(MASKED), r(TWO), const("first_e"), E, row[1], r(WEIGHT))
                    v.tensor_tensor(r(BOTH), r(ONE), r(TWO), ALU.add).then_inc(chosen, 1)
                    for i, x in enumerate((ONE, TWO)):
                        order.then(v.tensor_tensor(r(TMP), r(x), r(SCORE), ALU.mult))
                        order.then(v.tensor_reduce(share[:, i, :], r(TMP), AX, ALU.add))
                    order.then(v.tensor_tensor(row[2], share[:, 0, :], share[:, 1, :], ALU.add))
                    order.then(v.reciprocal(row[2], row[2]))
                    order.then(v.tensor_tensor(share[:], share[:], row[2].unsqueeze(1).to_broadcast((P, 2, TT)),
                                               ALU.mult))
                    v.wait_ge(counted, 1)
                    order.then(v.tensor_copy(r(RANK), ps[:, 1, 0:TT * E].rearrange("p (t e) -> p t e", e=E)))
                    cnt, more, cum, off = (count_f[:, i, :] for i in range(4))
                    order.then(v.tensor_copy(cnt, ps[:, 2, 0:E]))
                    order.then(v.tensor_scalar(more, cnt, float(P), None, ALU.is_gt))
                    for n in (2, 3):
                        order.then(v.tensor_scalar(cum, cnt, float(n * P), None, ALU.is_gt))
                        order.then(v.tensor_tensor(more, more, cum, ALU.add))
                    order.then(v.tensor_copy(cum, more))
                    s = 1
                    while s < E:
                        order.then(v.tensor_copy(off, cum))
                        order.then(v.tensor_tensor(cum[:, s:E], off[:, s:E], off[:, 0:E - s], ALU.add))
                        s *= 2
                    order.then(v.tensor_tensor(off, cum, more, ALU.subtract))
                    order.then(v.tensor_scalar(off, off, float(P), float((E - 1) * P), ALU.mult, ALU.add))
                    order.then(v.tensor_tensor(off, off, const("row0"), ALU.subtract))
                    order.then(v.tensor_scalar(r(TMP), r(RANK), float(P), None, ALU.is_ge))
                    order.then(v.tensor_tensor(r(DEST), r(TMP), over_t(off), ALU.mult))
                    order.then(v.tensor_tensor(r(DEST), r(DEST), r(RANK), ALU.add))
                    order.then(v.tensor_tensor(r(DEST), r(DEST), over_t(const("row0")), ALU.add))
                    for i, x in enumerate((ONE, TWO)):
                        order.then(v.tensor_tensor(r(TMP), r(x), r(DEST), ALU.mult))
                        order.then(v.tensor_reduce(slots_f[:, i, :], r(TMP), AX, ALU.add))
                    v.tensor_copy(slots[:], slots_f[:]).then_inc(slots_ready, 1)
                    order.then(v.tensor_tensor(over[:], cum.unsqueeze(1).to_broadcast((P, NBLK, E)),
                                               const("block").unsqueeze(2).to_broadcast((P, NBLK, E)), ALU.is_le))
                    order.then(v.tensor_reduce(block_f[:, 0:NBLK], over[:], AX, ALU.add))
                    order.then(v.tensor_tensor(block_f[:, 0:NBLK], block_f[:, 0:NBLK], const("own"), ALU.add))
                    order.then(v.tensor_scalar(block_f[:, 0:NBLK], block_f[:, 0:NBLK], float(E - 1), None, ALU.min))
                    order.then(v.tensor_scalar(block_f[:, NBLK:NBLK + 1], cum[:, E - 1:E], float(E), None, ALU.add))
                    order.then(v.tensor_copy(block_i[:], block_f[:]))

            chunks_e = [(m, n, kh) for n in range(2) for m in ("w1", "w3") for kh in range(2)] + \
                       [("w2", n, kh) for kh in range(2) for n in range(2)]
            ECH = len(chunks_e)
            assert ECH % NER == 0 and ECH % NEH == 0

            with nc.Block() as block:
                def blocks(engine, body):
                    n = engine.value_load(block_i[0:1, NBLK:NBLK + 1], min_val=E, max_val=E + OVF)
                    body(0, True)
                    with engine.Fori(1, n) as i:
                        body(i, False)

                @block.sync
                def _(sp):
                    def body(i, first):
                        if first:
                            e = 0
                        else:
                            e = sp.value_load(block_i[0:1, bass.ds(i, 1)], min_val=0, max_val=E - 1)
                        for j, (m, n, kh) in enumerate(chunks_e):
                            w = a[m][layer, e].rearrange("(k p) f -> p k f", p=P)[:, 4 * kh:4 * kh + 4,
                                                                                 n * 512:n * 512 + 512]
                            count = ECH * i + j + 1
                            if not first:
                                count = sp.snap(count)
                            sp.wait_ge(e_tails, count)
                            sp.dma_start(e_raw[j % NER][:], w).then_inc(e_raw_in[j % NER], 16)
                    blocks(sp, body)

                @block.gpsimd
                def _(pool):
                    pool.sem_inc(out_free, 1)
                    pool.dma_start(x_rows[:], slot_x[0:P, :]).then_inc(x_in, 16)

                    def body(i, first):
                        pool.wait_ge(e_turned, 4 * i + 2)
                        pool.dma_start(x_rows[:], slot_x[bass.ds((i + 1) * P, P), :]).then_inc(x_in, 16)
                        if not first:
                            pool.wait_ge(out_moved, i + 1)
                            pool.dma_start(slot_y[bass.ds((i - 1) * P, P), :], e_out[:].rearrange("p a b -> p (a b)"))\
                                .then_inc(y_stored, 16)
                            pool.wait_ge(y_stored, 16 * i)
                            pool.sem_inc(out_free, 1)
                    n = pool.value_load(block_i[0:1, NBLK:NBLK + 1], min_val=E, max_val=E + OVF)
                    body(0, True)
                    with pool.Fori(1, n) as i:
                        body(i, False)
                    pool.wait_ge(out_moved, n + 1)
                    pool.dma_start(slot_y[bass.ds((n - 1) * P, P), :], e_out[:].rearrange("p a b -> p (a b)"))\
                        .then_inc(y_stored, 16)
                    pool.wait_ge(y_stored, 16 * n)
                    pool.wait_ge(x_in, 16 * n + 16)

                @block.scalar
                def _(act):
                    def body(i, first):
                        def head(j):
                            act.wait_ge(e_raw_in[j % NER], 16 * (ECH // NER) * i + 16 * (j // NER + 1))
                            act.wait_ge(e_used, ECH * i + j + 1)
                            act.activation(e_head[j % NEH][:], e_raw[j % NER][:], ACT.Copy).then_inc(e_heads, 1)

                        def sigmoid(half):
                            act.wait_ge(e_used, ECH * i + 4 * half + 2 + NEH)
                            if not (first and half == 0):
                                act.wait_ge(gated, 2 * i + half + 2)
                            act.activation(e_sig[:], ps[:, 2 * half, :], ACT.Sigmoid).then_inc(sig_done, 1)

                        def turned(n, bank, to):
                            act.wait_ge(e_turned, 4 * i + 2 + n)
                            act.activation(to, ps[:, bank, :].rearrange("p (k s) -> p k s", s=P), ACT.Copy)\
                               .then_inc(e_t_heads, 1)

                        head(0)
                        head(1)
                        head(2)
                        if not first:
                            out_rows(i)
                        head(3)
                        head(4)
                        sigmoid(0)
                        head(5)
                        head(6)
                        head(7)
                        head(8)
                        turned(1, 6, aT_head[:, 0:4, :])
                        head(9)
                        sigmoid(1)
                        head(10)
                        turned(2, 7, xT_head[:, 0:4, :])
                        head(11)
                        turned(3, 6, xT_head[:, 4:8, :])
                        turned(4, 7, aT_head[:, 4:8, :])

                    def out_rows(i):
                        act.wait_ge(e_used, ECH * i + NEH)
                        act.wait_ge(out_free, i)
                        act.activation(e_out[:], ps[:, 4:6, :], ACT.Copy).then_inc(out_moved, 1)

                    act.sem_inc(out_moved, 1)
                    for q in range(2):
                        act.wait_ge(e_turned, q + 1)
                        act.activation(xT_head[:, 4 * q:4 * q + 4, :], ps[:, 6 + q, :].rearrange("p (k s) -> p k s", s=P),
                                       ACT.Copy).then_inc(e_t_heads, 1)
                    n = act.value_load(block_i[0:1, NBLK:NBLK + 1], min_val=E, max_val=E + OVF)
                    body(0, True)
                    with act.Fori(1, n) as i:
                        body(i, False)
                    out_rows(n)

                @block.vector
                def _(v):
                    def body(i, first):
                        def tail(j):
                            v.wait_ge(e_heads, ECH * i + j + 1)
                            v.tensor_tensor(e_tail[j % NEH][:], e_raw[j % NER][:], e_head[j % NEH][:], ALU.subtract)\
                             .then_inc(e_tails, 1)

                        def gated_half(half):
                            v.wait_ge(sig_done, 2 * i + half + 1)
                            v.wait_ge(e_used, ECH * i + 4 * half + 4 + NEH)
                            v.tensor_tensor(act_rows[:, half, :], ps[:, 2 * half, :], e_sig[:], ALU.mult)\
                             .then_inc(e_order, 1)
                            v.wait_ge(e_order, 2 * i + half + 1)
                            v.tensor_tensor(act_rows[:, half, :], ps[:, 2 * half + 1, :], act_rows[:, half, :], ALU.mult)\
                             .then_inc(gated, 1)

                        def turned(n, bank, head_, to):
                            v.wait_ge(e_t_heads, 4 * i + 2 + n)
                            v.tensor_tensor(to, ps[:, bank, :].rearrange("p (k s) -> p k s", s=P), head_, ALU.subtract)\
                             .then_inc(e_t_tails, 1)

                        for j in range(7):
                            tail(j)
                        gated_half(0)
                        tail(7)
                        tail(8)
                        turned(1, 6, aT_head[:, 0:4, :], aT_tail[:, 0:4, :])
                        tail(9)
                        gated_half(1)
                        tail(10)
                        turned(2, 7, xT_head[:, 0:4, :], xT_tail[:, 0:4, :])
                        tail(11)
                        turned(3, 6, xT_head[:, 4:8, :], xT_tail[:, 4:8, :])
                        turned(4, 7, aT_head[:, 4:8, :], aT_tail[:, 4:8, :])

                    v.sem_inc(e_tails, NER)
                    v.sem_inc(gated, 2)
                    for q in range(2):
                        v.wait_ge(e_t_heads, q + 1)
                        v.tensor_tensor(xT_tail[:, 4 * q:4 * q + 4, :], ps[:, 6 + q, :].rearrange("p (k s) -> p k s", s=P),
                                        xT_head[:, 4 * q:4 * q + 4, :], ALU.subtract).then_inc(e_t_tails, 1)
                    blocks(v, body)

                @block.tensor
                def _(pe):
                    ident = const("ident")

                    def turn(x, k0, bank):
                        for k in range(4):
                            i = nc.tensor.transpose(ps[:, bank, k * P:(k + 1) * P], x[:, (k0 + k) * P:(k0 + k + 1) * P],
                                                    ident)
                        i.then_inc(e_turned, 1)

                    def body(i, first):
                        acts = act_rows[:].rearrange("p a b -> p (a b)")
                        for j, (m, n, kh) in enumerate(chunks_e):
                            pe.wait_ge(e_tails, ECH * i + j + 1 + NER)
                            if m == "w2":
                                bank, (sh, st) = 4 + n, (aT_head, aT_tail)
                                if j == 8:
                                    pe.wait_ge(e_t_tails, 4 * i + 3)
                                    pe.wait_ge(out_moved, i + 1)
                                if j == 10:
                                    pe.wait_ge(e_t_tails, 4 * i + 6)
                            else:
                                bank, (sh, st) = 2 * n + (m == "w3"), (xT_head, xT_tail)
                                if j == 0:
                                    pe.wait_ge(e_t_tails, 4 * i + 2)
                                if j % 4 == 0:
                                    pe.wait_ge(gated, 2 * i + n + 1)
                            wh, wt = e_head[j % NEH], e_tail[j % NEH]
                            for k in range(4):
                                kk = 4 * kh + k
                                start, stop = kk == 0, kk == KD - 1
                                nc.tensor.matmul(ps[:, bank, :], sh[:, kk, :], wh[:, k, :], start=start, stop=False)
                                nc.tensor.matmul(ps[:, bank, :], sh[:, kk, :], wt[:, k, :], start=False, stop=False)
                                last = nc.tensor.matmul(ps[:, bank, :], st[:, kk, :], wh[:, k, :], start=False, stop=stop)
                                if j == 9 and k == 1:
                                    pe.wait_ge(gated, 2 * i + 4)
                                    pe.wait_ge(e_t_tails, 4 * i + 4)
                                    turn(acts, 4, 7)
                            last.then_inc(e_used, 1)
                            if j == 5:
                                pe.wait_ge(gated, 2 * i + 3)
                                pe.wait_ge(e_t_tails, 4 * i + 1)
                                turn(acts, 0, 6)
                            if j == 7:
                                pe.wait_ge(x_in, 16 * i + 32)
                                pe.wait_ge(e_t_tails, 4 * i + 2)
                                turn(x_rows, 0, 7)
                            if j == 8:
                                pe.wait_ge(e_t_tails, 4 * i + 3)
                                turn(x_rows, 4, 6)

                    pe.sem_inc(e_used, NEH)
                    pe.wait_ge(x_in, 16)
                    turn(x_rows, 0, 6)
                    turn(x_rows, 4, 7)
                    blocks(pe, body)

            with nc.Block() as block:
                @block.gpsimd
                def _(pool):
                    for i, rows in enumerate((rows1, rows2)):
                        for t in range(TT):
                            pool.indirect_dma_start(rows[:, t, :], None, slot_y[:, :],
                                                    bass.IndirectOffsetOnAxis(slots[:, i, t:t + 1], 0))\
                                .then_inc(gathered, 16)
                    pool.wait_ge(gathered, 16 * 2 * TT)

                @block.sync
                def _(sp):
                    for i, name in enumerate(("ln2_g", "ln2_b")):
                        sp.dma_start(ln2_gb[:, i, :], a[name][bass.ds(layer, 1), :].to_broadcast((P, D)))\
                          .then_inc(ln2_in, 16)
                    sp.wait_ge(h_final, 1)
                    sp.dma_start(out[0].rearrange("(t p) d -> p t d", p=P), h[:]).then_inc(h_stored, 16)
                    sp.wait_ge(h_stored, 16)

                @block.scalar
                def _(act):
                    act.wait_ge(var2_ready, 1)
                    act.activation(ln_sd, ln_mv[:, :, 1], ACT.Sqrt, bias=const("eps")[:, 0:1]).then_inc(root2_done, 1)

                @block.vector
                def _(v):
                    order = Steps(v, c_order)
                    v.wait_ge(gathered, 16 * 2 * TT)
                    for t in range(TT):
                        order.then(v.tensor_scalar(rows1[:, t, :], rows1[:, t, :], share[:, 0, t:t + 1], None, ALU.mult))
                        order.then(v.scalar_tensor_tensor(out=rows1[:, t, :], in0=rows2[:, t, :],
                                                          scalar=share[:, 1, t:t + 1], in1=rows1[:, t, :],
                                                          op0=ALU.mult, op1=ALU.add))
                        order.then(v.scalar_tensor_tensor(out=h[:, t, :], in0=h[:, t, :], scalar=ALPHA,
                                                          in1=rows1[:, t, :], op0=ALU.mult, op1=ALU.add))
                        layer_norm_stats(v, order, h[:, t, :], 2, ln_stats[:, t], ln_mv[:, t, :])
                    v.engine_nop().then_inc(var2_ready, 1)
                    v.wait_ge(root2_done, 1)
                    v.wait_ge(ln2_in, 32)
                    order.then(v.reciprocal(ln_sd, ln_sd))
                    for t in range(TT):
                        order.then(v.tensor_scalar(h[:, t, :], h[:, t, :], ln_mv[:, t, 0:1], ln_sd[:, t:t + 1],
                                                   ALU.subtract, ALU.mult))
                    order.then(v.tensor_tensor(h[:], h[:], ln2_gb[:, 0:1, :].to_broadcast((P, TT, D)), ALU.mult))
                    v.tensor_tensor(h[:], h[:], ln2_gb[:, 1:2, :].to_broadcast((P, TT, D)), ALU.add)\
                     .then_inc(h_final, 1)

            nc.gpsimd.dma_reset(range(sems[first_layer_sem].num, sems[-1].num + 1))
            nc.gpsimd.sem_clear(range(sems[first_layer_sem].num, sems[-1].num + 1))
            nc.all_engine_barrier()


INPUTS = ["x", "positions", "ln_in_g", "ln_in_b", "w_in", "conv_w", "sgu_ln_g", "sgu_ln_b", "w_s", "b_s",
          "lambda_q1", "lambda_k1", "lambda_q2", "lambda_k2", "diff_subln_g", "w_gate", "b_gate", "w_branch", "w_o",
          "ln1_g", "ln1_b", "w_router", "b_router", "w1", "w3", "w2", "ln2_g", "ln2_b"]


def kernel(**inputs):
    import concourse.bacc as bacc
    from concourse.bass_utils import run_bass_kernel_spmd

    nc = bacc.Bacc("TRN2", target_bir_lowering=False, num_devices=1)
    arrays = {name: np.ascontiguousarray(inputs[name]) for name in INPUTS}
    arrays["consts"], arrays["causal"], arrays["decay"] = constants()
    a = {name: nc.dram_tensor(f"in_{name}", x.shape, mybir.dt.from_np(x.dtype), kind="ExternalInput").ap()
         for name, x in arrays.items()}
    for name in ("slot_x", "slot_y"):
        a[name] = nc.dram_tensor(name, (NBLK * P, D), F32).ap()
    out = nc.dram_tensor("out", (1, T, D), F32, kind="ExternalOutput").ap()
    program(nc, a, out)
    r = run_bass_kernel_spmd(nc, [{f"in_{name}": x for name, x in arrays.items()}], core_ids=[0])
    return r.results[0]["out"]
```

```python
import math
from contextlib import ExitStack

import numpy as np
import concourse.bass as bass
from concourse import mybir
from concourse.alu_op_type import AluOpType as ALU

F32 = mybir.dt.float32
F32R = mybir.dt.float32r
I32 = mybir.dt.int32
ACT = mybir.ActivationFunctionType
AX = mybir.AxisListType.X

P = 128
D = 1024
T = 512
DEPTH = 2
KD = D // P
TT = T // P
W = 512
IN_COLS = 11 * W
E = 16
EG = 4
NG = 4
OVF = 7
NBLK = E + OVF + 1
ALPHA = (2.0 * DEPTH) ** 0.25
LN_EPS = 1e-5
RMS_EPS = 1e-6
NEG = -1e30
UP_TO = P + 4 * TT
EMPTY = 2048
AHEAD = 3
TWO_PI = 2 * math.pi

CONST = {}


def _const_layout():
    at = 0
    for name, n in (("ident", 128), ("swap_ret", 128), ("swap_diff", 128), ("upper", 128), ("strict", 128),
                    ("ones", 128), ("freq_ret", 1), ("freq_diff", 1), ("first_e", E),
                    ("expert", E), ("block", NBLK), ("lam", 2 * DEPTH), ("eps", 3)):
        CONST[name] = (at, at + n)
        at += n
    return at


NCONST = _const_layout()


def constants():
    c = np.zeros((P, NCONST), np.float32)

    def put(name, value):
        a, b = CONST[name]
        c[:, a:b] = value

    p = np.arange(P)
    put("ident", np.eye(P))
    for name, head, rot in (("swap_ret", 64, 64), ("swap_diff", 64, 16)):
        s = np.zeros((P, P))
        for m in range(P):
            d = m % head
            if d < rot // 2:
                s[m + rot // 2, m] = -1.0
            elif d < rot:
                s[m - rot // 2, m] = 1.0
        put(name, s)
    put("upper", p[None, :] >= p[:, None])
    put("strict", p[None, :] > p[:, None])
    put("ones", 1.0)
    f = np.float32
    inv_r = np.power(f(10000.0), -np.arange(32, dtype=f) / f(32)).astype(f)
    inv_d = np.power(f(500000.0), -np.arange(8, dtype=f) / f(8)).astype(f)
    put("freq_ret", inv_r[(p % 64) % 32][:, None])
    put("freq_diff", np.where(p % 64 < 16, inv_d[(p % 64) % 8], 0)[:, None])
    put("first_e", E - np.arange(E))
    put("expert", np.arange(E))
    put("block", np.arange(NBLK))
    lam = []
    for l in range(DEPTH):
        li = 0.8 - 0.6 * math.exp(-0.3 * l)
        lam += [li, 1.0 - li]
    put("lam", np.array(lam))
    put("eps", np.array([LN_EPS, RMS_EPS, math.pi / 2]))
    x = np.arange(T)
    mask = np.zeros((P, T), np.float32)
    mask[:, T - P:] = np.where(p[None, :] > p[:, None], NEG, 0.0)
    decay = np.zeros((4, P, T), np.float32)
    for h in range(4):
        lg = np.float32(np.log1p(-np.exp2(np.float32(-5.0 - h))))
        rel = (x[None, :] - p[:, None]).astype(np.float32)
        decay[h] = np.where(rel >= 0, np.exp(np.maximum(rel, 0) * lg) * 0.125, 0.0)
    token = np.arange(TT)[None, :] * P + p[:, None]
    dispatch = np.zeros((P, UP_TO + E * E), np.float32)
    dispatch[:, UP_TO:] = np.tril(np.ones((E, E))).reshape(1, -1)
    dispatch[:, 0:P] = p[None, :]
    rows = dispatch[:, P:UP_TO].reshape(P, 2, TT, 2)
    for choice in range(2):
        rows[:, choice, :, 0] = token - EMPTY
        rows[:, choice, :, 1] = token + choice * T - EMPTY
    return c, mask, decay, dispatch


CONV, DIFF, RET, SGU = 0, 3, 1, 2
GROUPS = {
    CONV: [("T", 0), ("T", 1), ("T", 2)],
    DIFF: [("T", 8), ("T", 9), ("N", 10)],
    RET: [("T", 3), ("N", 4), ("T", 5)],
    SGU: [("T", 6), ("N", 7)],
}
ZBUF = {CONV: 1, DIFF: 0, RET: 1, SGU: 0}
ORDER = [CONV, DIFF, RET, SGU]


def dense_plan():
    chunks = []

    def project(b):
        for g, (kind, tile) in enumerate(GROUPS[b]):
            for half in range(2):
                chunks.append(dict(kind="Z" + kind, b=b, g=g, tile=tile, half=half, units=[]))

    def gates(b):
        for q in range(4):
            chunks.append(dict(kind="gate", b=b, q=q, units=[]))
            chunks.append(dict(kind="branch", b=b, q=q, units=[]))

    project(CONV)
    project(DIFF)
    gates(CONV)
    project(RET)
    gates(DIFF)
    project(SGU)
    gates(RET)
    gates(SGU)
    for n in range(2):
        for half in range(2):
            chunks.append(dict(kind="wo", n=n, half=half, units=[]))

    def where(kind, b):
        return [c for c, x in enumerate(chunks) if x["kind"].startswith(kind) and x.get("b") == b]

    def at(slot, *unit):
        c, end = slot
        chunks[c]["units" if end else "mid"].append(unit)

    def halves(cs):
        return [(c, end) for c in cs for end in (0, 1)]

    def spread(slots, gaps):
        length = {c: 24 if chunks[c]["kind"] == "branch" else 48 for c, _ in slots}
        at_end, t = [], 0
        for c, end in slots:
            t += length[c] / 2
            at_end.append(t)
        first, scale = at_end[0], (at_end[-1] - at_end[0]) / sum(gaps)
        found, target, n = [slots[0]], first, 0
        for gap in gaps:
            target += gap * scale
            while n < len(slots) - 1 and at_end[n] < target - 6:
                n += 1
            found.append(slots[n])
        return found

    for x in chunks:
        x["mid"] = []
    zd, zr, zs = (where("Z", b) for b in (DIFF, RET, SGU))
    gc, gd, gr, gs = (sorted(where("gate", b) + where("branch", b)) for b in ORDER)

    for m in range(4):
        at((zd[m], 1), "conv", m)
    at((gc[0] - 1, 1), "split", CONV)
    at((zd[2], 0), "rotate", DIFF, 0)
    at((zd[4], 0), "rotate", DIFF, 1)
    slots = [(gc[0] - 1, 1)] + halves(gc + zr)[:-1]
    units = 4 * TT
    placed = spread(slots, [2.5 + u % TT for u in range(units)] + [3, 3])
    for u, slot in enumerate(placed):
        if u >= TT + 1 and (u - 1) % TT == 0:
            at(slot, "diff_values", (u - 1) // TT - 1)
        if 0 < u <= units:
            at(slot, "diff_transpose", u - 1)
        if u < units:
            at(slot, "diff_scores", u)
        if u >= TT + 2 and (u - 2) % TT == 0:
            at(slot, "diff_norm", (u - 2) // TT - 1)
    at((gd[0] - 1, 1), "split", DIFF)
    slots = halves(gd + zs)[:-1]
    steps = [("rotate", RET, 0)] + [(k, h) for h in range(4) for k in ("ret_scores", "ret_values", "ret_norm")]
    after = {"rotate": 5, "ret_scores": 4, "ret_values": 2, "ret_norm": 5}
    for slot, unit in zip(spread(slots, [after[step[0]] for step in steps[:-1]]), steps):
        at(slot, *unit)
    at((gr[0] - 1, 1), "split", RET)
    at((gr[0], 1), "sgu_mask")
    for n in range(TT):
        at((gr[1 + n], 1), "sgu_norm", n)
    at((gr[6], 0), "sgu_mix")
    at((gs[0] - 1, 1), "split", SGU)
    for q in range(3):
        at((gs[-1], 0), "merge_split", q)
    at((gs[-1], 1), "merge_split", 3)
    return chunks


class Steps:

    def __init__(self, engine, done):
        self.engine, self.done, self.count = engine, done, 0

    def then(self, instruction):
        self.count += 1
        instruction.then_inc(self.done, 1)
        self.engine.wait_ge(self.done, self.count)


class RowNorm:

    def __init__(self, name, sem, h, stats, mean_var, root, shift):
        self.h, self.stats, self.mv, self.root, self.shift = h, stats, mean_var, root, shift
        self.var_ready, self.root_ready = sem(name + "_var_ready"), sem(name + "_root_ready")
        self.scale_ready, self.scaled = sem(name + "_scale_ready"), sem(name + "_scaled")
        self.gained, self.ready = sem(name + "_gained"), sem(name + "_ready")

    def vector(self, v, order, before, gain, after=None):
        h, mv, root, shift = self.h, self.mv, self.root, self.shift

        def variance(t):
            before(v, order, t)
            v.bn_stats(self.stats[:, t, 0, :], h[:, t, 0:512])
            order.then(v.bn_stats(self.stats[:, t, 1, :], h[:, t, 512:1024]))
            v.bn_aggr(mv[:, t, :], self.stats[:, t].rearrange("p a b -> p (a b)")).then_inc(self.var_ready, 1)

        def scale(t):
            v.wait_ge(self.root_ready, t + 1)
            order.then(v.reciprocal(root[:, t:t + 1], root[:, t:t + 1]))
            v.scalar_tensor_tensor(out=shift[:, t:t + 1], in0=mv[:, t, 0:1], scalar=-1.0, in1=root[:, t:t + 1],
                                   op0=ALU.mult, op1=ALU.mult).then_inc(self.scale_ready, 1)

        def gained(t):
            v.wait_ge(self.scaled, t + 1)
            v.tensor_tensor(h[:, t, :], h[:, t, :], gain, ALU.mult).then_inc(self.gained, 1)

        variance(0)
        variance(1)
        scale(0)
        variance(2)
        scale(1)
        gained(0)
        variance(3)
        scale(2)
        gained(1)
        scale(3)
        gained(2)
        gained(3)
        if after:
            for t in range(TT):
                after(v, t)

    def scalar(self, act, eps, before=None):
        def root(t):
            if before:
                before(act, t)
            act.wait_ge(self.var_ready, t + 1)
            act.activation(self.root[:, t:t + 1], self.mv[:, t, 1:2], ACT.Sqrt, bias=eps).then_inc(self.root_ready, 1)

        def scaled(t):
            act.wait_ge(self.scale_ready, t + 1)
            act.activation(self.h[:, t, :], self.h[:, t, :], ACT.Identity, bias=self.shift[:, t:t + 1],
                           scale=self.root[:, t:t + 1]).then_inc(self.scaled, 1)

        root(0)
        root(1)
        scaled(0)
        root(2)
        scaled(1)
        root(3)
        scaled(2)
        scaled(3)

    def gpsimd(self, pool, bias):
        for t in range(TT):
            pool.wait_ge(self.gained, t + 1)
            pool.tensor_tensor(self.h[:, t, :], self.h[:, t, :], bias, ALU.add).then_inc(self.ready, 1)


class LayerStart:

    def __init__(self, name, sem, norm, ps, ident, chunk, h, hT):
        self.norm, self.ps, self.ident, self.h = norm, ps, ident, h
        self.raw, self.head, self.tail = chunk
        self.hT_head, self.hT_tail = hT
        self.landed, self.head_made, self.tail_made = (sem(name + "_landed"), sem(name + "_head_made"),
                                                       sem(name + "_tail_made"))
        self.turned, self.heads, self.tails = sem(name + "_turned"), sem(name + "_heads"), sem(name + "_tails")

    def banks(self, t):
        return self.ps[:, 2 * t:2 * t + 2, :].rearrange("p a (k i) -> p (a k) i", i=P)

    def sync(self, sp, source):
        sp.dma_start(self.raw, source).then_inc(self.landed, 16)

    def tensor(self, pe):
        for t in range(TT):
            pe.wait_ge(self.norm.ready, t + 1)
            for k in range(KD):
                i = pe.transpose(self.ps[:, 2 * t + k // 4, (k % 4) * P:(k % 4 + 1) * P],
                                 self.h[:, t, k * P:(k + 1) * P], self.ident)
            i.then_inc(self.turned, 1)

    def scalar_chunk(self, act):
        act.wait_ge(self.landed, 16)
        act.activation(self.head, self.raw, ACT.Copy).then_inc(self.head_made, 1)

    def scalar(self, act):
        for t in range(TT):
            act.wait_ge(self.turned, t + 1)
            act.activation(self.hT_head[:, :, t * P:(t + 1) * P], self.banks(t), ACT.Copy).then_inc(self.heads, 1)

    def gpsimd(self, pool):
        pool.wait_ge(self.head_made, 1)
        pool.tensor_tensor(self.tail, self.raw, self.head, ALU.subtract).then_inc(self.tail_made, 1)

    def vector(self, v, t):
        v.wait_ge(self.heads, t + 1)
        v.tensor_tensor(self.hT_tail[:, :, t * P:(t + 1) * P], self.banks(t), self.hT_head[:, :, t * P:(t + 1) * P],
                        ALU.subtract).then_inc(self.tails, 1)


def program(nc, a, out):
    plan = dense_plan()
    nchunk = len(plan)
    c_of = {}
    for c, x in enumerate(plan):
        for unit in x["mid"] + x["units"]:
            c_of[unit] = c

    origin = -(-nc.sbuf_base // 32) * 32
    place = [0]

    def sb(name, shape, dt=F32, at=None):
        size = 4 * int(np.prod(shape[1:]))
        offset = place[0] if at is None else at
        if at is None:
            place[0] += -(-size // 32) * 32
        t = nc.alloc_sbuf_tensor_at(name, shape, dt, offset=origin + offset)
        return t

    consts = sb("consts", [P, NCONST])

    def const(name, rows=P):
        lo, hi = CONST[name]
        return consts[0:rows, lo:hi]

    ln_stats = sb("ln_stats", [P, TT, 2, 6])
    ln_mv = sb("ln_mv", [P, TT, 2])
    small = sb("small", [P, 18])
    lam_in, lam, top, rowsum = small[:, 0:2], small[:, 2:6], small[:, 6:8], small[:, 8:10]
    ln_sd, ln_shift = small[:, 10:14], small[:, 14:18]
    z0_at = place[0]
    z0 = sb("z0", [P, 3, TT, W])
    h = sb("h", [P, TT, D], at=z0_at)
    spare_at = z0_at + 4 * TT * D
    act_rows = sb("act_rows", [P, 2, 512], at=spare_at)
    e_out = sb("e_out", [P, D], at=spare_at + 4 * D)
    shared = place[0]
    tables = sb("tables", [P, 5, T])
    cos_ret, sin_ret, cos_diff, sin_diff, causal = (tables[:, i, :] for i in range(5))
    z1_at = place[0]
    z1 = sb("z1", [P, 3, TT, W])
    z = {0: z0, 1: z1}
    hT_at = place[0]
    hT_head, hT_tail = sb("hT_head", [P, KD, T], F32R), sb("hT_tail", [P, KD, T], F32R)
    merged_at = place[0]
    merged = sb("merged", [P, KD, T])
    yT_head, yT_tail = sb("yT_head", [P, 4, T], F32R), sb("yT_tail", [P, 4, T], F32R)
    NRAW, NHEAD = 4, 3
    ring_at = place[0]
    w_head = [sb(f"w_head{i}", [P, 2048], F32R) for i in range(NHEAD)]
    raw_at = [ring_at + 4 * 2048 * i for i in (6, 3, 4, 5)]
    raw = [sb(f"raw{i}", [P, 2048], at=raw_at[i]) for i in range(NRAW)]
    w_tail = [sb(f"w_tail{i}", [P, 2048], F32R, at=raw_at[i]) for i in range(NRAW)]
    place[0] += NRAW * 4 * 2048
    att_at = place[0]
    att = sb("att", [P, 2, T])
    attT = sb("attT", [P, TT, T])
    decay = sb("decay", [P, 2, T])
    gate = sb("gate", [P, 2, T])
    square_at = place[0]
    square = sb("square", [P, T])
    std = sb("std", [P, T])
    silu = sb("silu", [P, T])
    prow = sb("prow", [45, P], at=square_at)
    prm = sb("prm", [P, 45])
    lam_rows = sb("lam_rows", [P, 4, 64], at=square_at + 4 * P)
    assert origin + place[0] <= nc.sbuf_usable_end, origin + place[0] - nc.sbuf_usable_end

    place[0] = shared
    route = sb("route", [P, 24, TT * E])
    w_router = sb("w_router", [P, KD, E])
    b_router = sb("b_router", [P, E])
    slot_of, block_of = sb("slot_of", [P, 2 * TT]), sb("block_of", [P, 2 * TT])
    share = sb("share", [P, 2, TT])
    count_f = sb("count_f", [P, 4, E])
    over = sb("over", [P, NBLK, E])
    sums = sb("sums", [P, E, E])
    block_f = sb("block_f", [P, NBLK + 2])
    block_i = sb("block_i", [P, NBLK + 2], I32)
    slot_table = sb("slot_table", [P, 2, NBLK], I32)
    x_index, y_index = sb("x_index", [P, 1], I32), sb("y_index", [P, 1], I32)
    x_rows = sb("x_rows", [P, D])
    slot_hot = sb("slot_hot", [P, 2 * TT, P], F32R, at=place[0])
    logits_T = sb("logits_T", [E, T], at=place[0])
    ln2_gb = sb("ln2_gb", [P, 2, D], at=place[0])
    xT_head, xT_tail = sb("xT_head", [P, KD, P], F32R), sb("xT_tail", [P, KD, P], F32R)
    row_hot = sb("row_hot", [P, 2 * TT, 2, NBLK], F32R, at=place[0])
    block_hot = sb("block_hot", [P, 2 * TT, NBLK], at=place[0] + 16 * TT * NBLK)
    dispatch = sb("dispatch", [P, UP_TO + E * E], at=place[0] + 24 * TT * NBLK)
    assert 4 * (6 * TT * NBLK + UP_TO + E * E) <= 4096
    e_sig = sb("e_sig", [P, 2, 512])
    assert place[0] <= z1_at + 4 * 3 * TT * W, place[0]
    NEH = 3
    ln1_gb = sb("ln1_gb", [P, 2, D], at=place[0])
    aT_head, aT_tail = sb("aT_head", [P, KD, P], F32R), sb("aT_tail", [P, KD, P], F32R)
    CHUNK = 8 * D
    assert place[0] <= hT_at
    e_head = [sb(f"e_head{i}", [P, 2, D], F32R, at=ring_at + i * CHUNK) for i in range(NEH)]
    e_tail = [sb(f"e_tail{i}", [P, 2, D], F32R, at=ring_at + (NEH + i) * CHUNK) for i in range(NEH)]
    early = [merged_at + i * CHUNK for i in range(4)] + [att_at + i * CHUNK for i in range(3)]
    e_raw_at = early + [ring_at + 6 * CHUNK] + [hT_at + i * CHUNK for i in range(4)]
    NER, EARLY = len(e_raw_at), len(early)
    e_raw = [sb(f"e_raw{i}", [P, 2, D], at=e_raw_at[i]) for i in range(NER)]
    hT = sb("hT", [P, KD, T], at=e_raw_at[NER - 2])
    rows1 = sb("rows1", [P, TT, D], at=merged_at)
    rows2 = sb("rows2", [P, TT, D], at=merged_at + 4 * TT * D)
    diag = sb("diag", [P, TT, 2, P], at=ring_at + CHUNK)

    h1_rows = a["h1_rows"]
    y_rows = a["y_rows"]
    out_tiles = out[0].rearrange("(t p) d -> p t d", p=P)

    with ExitStack() as ctx:
        ps = ctx.enter_context(nc.psum_tensor("ps", [P, 8, 512], F32))
        sems = []

        def sem(name):
            s = ctx.enter_context(nc.semaphore(name))
            sems.append(s)
            return s

        def is_narrow(x):
            return x["kind"] in ("ZT", "gate", "branch")

        def wide_bank(x):
            return 4 * x["n"] if x["kind"] == "wo" else 0

        def raw_view(buf, x):
            if x["kind"] == "branch":
                return buf[:, 0:1024].rearrange("p (k n) -> p k n", k=4)
            if is_narrow(x):
                return buf[:, :].rearrange("p (k n) -> p k n", k=8)
            return buf[:, :].rearrange("p (k n) -> p k n", k=4)

        def projection_columns(layer, tile, half):
            c0 = tile * W + half * 256
            return a["w_in"][layer].rearrange("(k p) n -> p k n", p=P)[:, :, c0:c0 + 256]

        assert plan[0]["kind"] == "ZT"
        first_chunk = tuple(raw_view(x[0], plan[0]) for x in (raw, w_head, w_tail))

        in_ready = [sem(f"in_ready{t}") for t in range(TT)]
        gb_ready, pos_ready = sem("gb_ready"), sem("pos_ready")
        dve_done, angle_ready, sin_done = sem("dve_done"), sem("angle_ready"), sem("sin_done")
        abs_ready = sem("abs_ready")
        norm0 = RowNorm("norm0", sem, h, ln_stats, ln_mv, ln_sd, ln_shift)
        start0 = LayerStart("start0", sem, norm0, ps, const("ident"), first_chunk, h, (hT_head, hT_tail))
        setup_sems = list(sems)
        x_saved, tables_saved = sem("x_saved"), sem("tables_saved")
        gb_at = merged_at
        gb = sb("gb", [P, 2, D], at=gb_at)
        pos_i = sb("pos_i", [P, T], I32, at=gb_at + 8 * D)
        ang = sb("ang", [P, 2, 2, T], at=gb_at + 8 * D + 4 * T)
        turns_i = sb("turns_i", [P, 2, T], I32, at=gb_at + 8 * D + 20 * T)
        turns = sb("turns", [P, 2, T], at=gb_at + 8 * D + 28 * T)
        posf = sb("posf", [P, T], at=gb_at + 8 * D + 36 * T)

        with nc.Block() as block:
            @block.sync
            def _(sp):
                sp.dma_start(consts[:], a["consts"][:, :]).then_inc(pos_ready, 16)
                for t in range(TT):
                    sp.dma_start(h[:, t, :], a["x"][0, t * P:(t + 1) * P, :]).then_inc(in_ready[t], 16)
                for i, name in enumerate(("ln_in_g", "ln_in_b")):
                    sp.dma_start(gb[:, i, :], a[name].rearrange("(a d) -> a d", a=1).to_broadcast((P, D)))\
                      .then_inc(gb_ready, 16)
                start0.sync(sp, projection_columns(0, plan[0]["tile"], plan[0]["half"]))
                sp.dma_start(pos_i[:], a["positions"][0:1, :].to_broadcast((P, T))).then_inc(pos_ready, 16)
                for t in range(TT):
                    sp.wait_ge(norm0.ready, t + 1)
                    sp.dma_start(out_tiles[:, t, :], h[:, t, :]).then_inc(x_saved, 16)
                sp.wait_ge(sin_done, 2)
                sp.dma_start(a["tables"][:, 0:4, :], tables[:, 0:4, :]).then_inc(tables_saved, 16)

            @block.gpsimd
            def _(pool):
                norm0.gpsimd(pool, gb[:, 1, :])
                start0.gpsimd(pool)

            @block.tensor
            def _(pe):
                start0.tensor(pe)

            @block.scalar
            def _(act):
                norm0.scalar(act, const("eps")[:, 0:1])
                start0.scalar_chunk(act)
                start0.scalar(act)
                act.wait_ge(angle_ready, 1)
                act.activation(ang[:, :, 1, :], ang[:, :, 0, :], ACT.Abs).then_inc(abs_ready, 1)
                act.wait_ge(abs_ready, 1)
                for i, (co, si) in enumerate(((cos_ret, sin_ret), (cos_diff, sin_diff))):
                    act.activation(si, ang[:, i, 0, :], ACT.Sin)
                    act.activation(co, ang[:, i, 1, :], ACT.Sin, scale=-1.0, bias=const("eps")[:, 2:3])\
                       .then_inc(sin_done, 1)

            @block.vector
            def _(v):
                order = Steps(v, dve_done)

                def landed(v, order, t):
                    v.wait_ge(in_ready[t], 16)
                    if t == 2:
                        v.wait_ge(gb_ready, 32)

                norm0.vector(v, order, landed, gb[:, 0, :])
                v.wait_ge(pos_ready, 32)
                order.then(v.tensor_copy(posf[:], pos_i[:]))
                for i, f in enumerate(("freq_ret", "freq_diff")):
                    last = v.tensor_scalar(ang[:, i, 0, :], posf[:], const(f), None, ALU.mult)
                order.then(last)
                order.then(v.tensor_scalar(turns[:], ang[:, :, 0, :], 1.0 / TWO_PI, None, ALU.mult))
                order.then(v.tensor_copy(turns_i[:], turns[:]))
                order.then(v.tensor_copy(turns[:], turns_i[:]))
                c1 = 6.28125
                c2 = float(np.float32(round((TWO_PI - c1) * 2 ** 20) / 2 ** 20))
                c3 = TWO_PI - c1 - c2
                for c in (c1, c2, c3):
                    order.then(v.scalar_tensor_tensor(out=ang[:, :, 0, :], in0=turns[:], scalar=-c,
                                                      in1=ang[:, :, 0, :], op0=ALU.mult, op1=ALU.add))
                v.tensor_scalar(ang[:, :, 0, :], ang[:, :, 0, :], 3.1415925, -3.1415925, ALU.min, ALU.max)\
                 .then_inc(angle_ready, 1)
                for t in range(TT):
                    start0.vector(v, t)
        first_layer_sem = len(sems)

        raw_in = [sem(f"raw_in{i}") for i in range(NRAW)]
        heads, tails, chunk_used = sem("heads"), sem("tails"), sem("chunk_used")
        z_moved, gates_done, merged_done = sem("z_moved"), sem("gates_done"), sem("merged_done")
        params_in, prm_turned, prm_ready = sem("params_in"), sem("prm_turned"), sem("prm_ready")
        lam_exp_in, lam_exp = sem("lam_exp_in"), sem("lam_exp")
        swapped, rotated = sem("swapped"), sem("rotated")
        scores_ready, masked, exps_done, att_ready = (sem("scores_ready"), sem("masked"), sem("exps_done"),
                                                      sem("att_ready"))
        att_turned, att_copied, values_ready = sem("att_turned"), sem("att_copied"), sem("values_ready")
        squared, summed, rooted, normed = sem("squared"), sem("summed"), sem("rooted"), sem("normed")
        decay_in = [sem("decay_in0"), sem("decay_in1")]
        ret_scores_ready, decayed, ret_values_ready = (sem("ret_scores_ready"), sem("decayed"),
                                                       sem("ret_values_ready"))
        silu_ready = sem("silu_ready")
        ws_in, tables_in, ws_turned, ws_masked = sem("ws_in"), sem("tables_in"), sem("ws_turned"), sem("ws_masked")
        var_ready, sgu_root, sgu_normed, mixed_ready = (sem("var_ready"), sem("sgu_root"), sem("sgu_normed"),
                                                        sem("mixed_ready"))
        conv_done, sgu_done = sem("conv_done"), sem("sgu_done")
        y_heads, y_tails, m_heads, m_tails = sem("y_heads"), sem("y_tails"), sem("m_heads"), sem("m_tails")
        h_back, ln1_in, summed_out, out_tile = sem("h_back"), sem("ln1_in"), sem("summed_out"), sem("out_tile")
        tables_back = sem("tables_back")
        norm1 = RowNorm("norm1", sem, h, ln_stats, ln_mv, ln_sd, ln_shift)
        denssig_times = sem("denssig_times")
        router_in, r_turned, r_copied, logits_ready = (sem("router_in"), sem("r_turned"), sem("r_copied"),
                                                       sem("logits_ready"))
        r_shift, r_exp, chosen, counted, hot_ready, table_made, table_ready, blocks_ready = (
            sem("r_shift"), sem("r_exp"), sem("chosen"), sem("counted"), sem("hot_ready"), sem("table_made"),
            sem("table_ready"), sem("blocks_ready"))
        logits_made, logits_copied = sem("logits_made"), sem("logits_copied")
        h1_saved, x_cleared = sem("h1_saved"), sem("x_cleared")
        e_raw_in = [sem(f"e_raw_in{i}") for i in range(NER)]
        e_heads, e_tails, e_used = sem("e_heads"), sem("e_tails"), sem("e_used")
        index_ready, x_in, e_turned, e_t_heads, e_t_tails = (sem("index_ready"), sem("x_in"), sem("e_turned"),
                                                             sem("e_t_heads"), sem("e_t_tails"))
        sig_done, gated, out_moved, y_stored, out_free = (sem("sig_done"), sem("gated"), sem("out_moved"),
                                                          sem("y_stored"), sem("out_free"))
        sig_times, index_seen, queue_short = sem("sig_times"), sem("index_seen"), sem("queue_short")
        y1_in = [sem(f"y1_in{t}") for t in range(TT)]
        y2_in = [sem(f"y2_in{t}") for t in range(TT)]
        ln2_in, y_summed, c_order, h_stored = sem("ln2_in"), sem("y_summed"), sem("c_order"), sem("h_stored")
        diag_made = sem("diag_made")
        norm2 = RowNorm("norm2", sem, h, ln_stats, ln_mv, ln_sd, ln_shift)
        start2 = LayerStart("start2", sem, norm2, ps, const("ident"), first_chunk, h, (hT_head, hT_tail))

        for s in setup_sems:
            nc.gpsimd.sem_clear(s)
        nc.all_engine_barrier()

        free_by, n_z, n_gate, n_merge, n_out = [], 0, 0, 0, 0
        for x in plan:
            if x["kind"] == "ZT":
                n_z += 1
                free_by.append((z_moved, n_z))
            elif x["kind"] == "ZN":
                n_z += x["half"]
                free_by.append((z_moved, n_z + 1 - x["half"]))
            elif x["kind"] == "gate":
                n_gate += 1
                free_by.append((gates_done, n_gate))
            elif x["kind"] == "branch":
                n_merge += 1
                free_by.append((merged_done, n_merge))
            else:
                n_out += x["half"]
                free_by.append((summed_out, n_out + 1 - x["half"]))
        z_count = {}
        n = 0
        for x in plan:
            if x["kind"] == "ZT" or (x["kind"] == "ZN" and x["half"]):
                n += 1
                z_count[(x["b"], x["g"], x["half"])] = n
        z_all = {b: max(v for k, v in z_count.items() if k[0] == b) for b in ORDER}
        gate_chunk = {b: [c for c, x in enumerate(plan) if x["kind"] == "gate" and x["b"] == b] for b in ORDER}
        y_of = {CONV: z1[:, 2], DIFF: z0[:, 0], RET: z1[:, 2], SGU: z0[:, 0]}
        y_done = {CONV: (conv_done, 4), DIFF: (normed, 4), RET: (normed, 8), SGU: (sgu_done, 1)}
        turned_before_norm = {hd: min(4 * TT, (hd + 1) * TT + 2) for hd in range(4)}

        with nc.Fori(0, DEPTH) as layer:
            def r(i):
                return route[:, i, :].rearrange("p (t e) -> p t e", e=E)

            def over_e(x):
                return x.unsqueeze(2).to_broadcast((P, TT, E))

            def over_t(x, n=E):
                return x.unsqueeze(1).to_broadcast((P, TT, n))

            LOGIT, SCORE, SEL, MASKED, WEIGHT, ONE, TWO, BOTH, RANK, BLOCK, TMP = range(11)
            PAIR = MASKED

            def router(v, order):
                pairs = [route[:, 12 + i, 0:TT * NG] for i in range(8)]
                row = [route[:, 20 + i, 0:TT] for i in range(4)]

                def first_max(src, onehot, by, n, top_, weights):
                    b3 = (P, TT, n)
                    order.then(v.tensor_reduce(top_, src, AX, ALU.max))
                    order.then(v.tensor_tensor(weights, src, top_.unsqueeze(2).to_broadcast(b3), ALU.is_equal))
                    order.then(v.tensor_tensor(weights, weights, over_t(by, n), ALU.mult))
                    order.then(v.tensor_reduce(top_, weights, AX, ALU.max))
                    order.then(v.tensor_tensor(onehot, weights, top_.unsqueeze(2).to_broadcast(b3), ALU.is_equal))

                v.wait_ge(router_in, 48)
                v.wait_ge(logits_ready, 1)
                order.then(v.tensor_copy(r(LOGIT), ps[:, 1, 0:TT * E].rearrange("p (t e) -> p t e", e=E)))
                order.then(v.tensor_reduce(row[0], r(LOGIT), AX, ALU.max))
                v.tensor_tensor(r(LOGIT), r(LOGIT), over_e(row[0]), ALU.subtract).then_inc(r_shift, 1)
                v.wait_ge(r_exp, 1)
                order.then(v.tensor_reduce(row[0], r(SCORE), AX, ALU.add))
                order.then(v.reciprocal(row[0], row[0]))
                order.then(v.tensor_tensor(r(SCORE), r(SCORE), over_e(row[0]), ALU.mult))
                order.then(v.tensor_tensor(r(SEL), r(SCORE), over_t(b_router[:, :]), ALU.add))
                s4 = route[:, SEL, :].rearrange("p (g e) -> p g e", e=EG)
                hi1, lo1, hi2, lo2, t1, t2 = pairs[:6]
                v.tensor_tensor(hi1, s4[:, :, 0], s4[:, :, 1], ALU.max)
                v.tensor_tensor(lo1, s4[:, :, 0], s4[:, :, 1], ALU.min)
                v.tensor_tensor(hi2, s4[:, :, 2], s4[:, :, 3], ALU.max)
                order.then(v.tensor_tensor(lo2, s4[:, :, 2], s4[:, :, 3], ALU.min))
                v.tensor_tensor(t1, hi1, hi2, ALU.max)
                v.tensor_tensor(t2, hi1, hi2, ALU.min)
                order.then(v.tensor_tensor(lo1, lo1, lo2, ALU.max))
                order.then(v.tensor_tensor(t2, t2, lo1, ALU.max))
                order.then(v.tensor_tensor(t1, t1, t2, ALU.add))
                g3 = t1.rearrange("p (t g) -> p t g", g=NG)
                best = t2.rearrange("p (t g) -> p t g", g=NG)
                first_max(g3, best, const("first_e")[:, E - NG:E], NG, row[1], hi1.rearrange("p (t g) -> p t g", g=NG))
                m4 = route[:, MASKED, :].rearrange("p (g e) -> p g e", e=EG)
                order.then(v.tensor_scalar(t2, t2, -NEG, NEG, ALU.mult, ALU.add))
                order.then(v.tensor_tensor(m4, s4, t2.unsqueeze(2).to_broadcast((P, TT * NG, EG)), ALU.add))
                first_max(r(MASKED), r(ONE), const("first_e"), E, row[1], r(WEIGHT))
                order.then(v.scalar_tensor_tensor(out=r(MASKED), in0=r(ONE), scalar=3 * NEG, in1=r(MASKED),
                                                  op0=ALU.mult, op1=ALU.add))
                first_max(r(MASKED), r(TWO), const("first_e"), E, row[1], r(WEIGHT))
                v.tensor_tensor(r(BOTH), r(ONE), r(TWO), ALU.add).then_inc(chosen, 1)
                for i, x in enumerate((ONE, TWO)):
                    order.then(v.tensor_tensor(r(TMP), r(x), r(SCORE), ALU.mult))
                    order.then(v.tensor_reduce(share[:, i, :], r(TMP), AX, ALU.add))
                order.then(v.tensor_tensor(row[2], share[:, 0, :], share[:, 1, :], ALU.add))
                order.then(v.reciprocal(row[2], row[2]))
                order.then(v.tensor_tensor(share[:], share[:], row[2].unsqueeze(1).to_broadcast((P, 2, TT)),
                                           ALU.mult))
                v.wait_ge(counted, 1)
                totals = ps[:, 2, 0:TT * E].rearrange("p (t e) -> p t e", e=E)
                within = ps[:, 1, 0:TT * E].rearrange("p (t e) -> p t e", e=E)
                cnt, more, cum, off = (count_f[:, i, :] for i in range(4))
                order.then(v.tensor_copy(r(TMP)[:, 1, :], totals[:, 0, :]))
                order.then(v.tensor_tensor(r(TMP)[:, 2, :], r(TMP)[:, 1, :], totals[:, 1, :], ALU.add))
                order.then(v.tensor_tensor(r(TMP)[:, 3, :], r(TMP)[:, 2, :], totals[:, 2, :], ALU.add))
                v.tensor_copy(r(RANK)[:, 0, :], within[:, 0, :])
                order.then(v.tensor_tensor(cnt, r(TMP)[:, 3, :], totals[:, 3, :], ALU.add))
                order.then(v.tensor_tensor(r(RANK)[:, 1:TT, :], r(TMP)[:, 1:TT, :], within[:, 1:TT, :], ALU.add))
                v.tensor_scalar(more, cnt, float(P), None, ALU.is_gt)
                order.then(v.tensor_scalar(r(TMP), r(RANK), float(P), None, ALU.is_ge))
                for n in (2, 3):
                    v.scalar_tensor_tensor(out=more, in0=cnt, scalar=float(n * P), in1=more, op0=ALU.is_gt, op1=ALU.add)
                    order.then(v.scalar_tensor_tensor(out=r(TMP), in0=r(RANK), scalar=float(n * P), in1=r(TMP),
                                                      op0=ALU.is_ge, op1=ALU.add))
                v.tensor_tensor(sums[:], more.unsqueeze(1).to_broadcast((P, E, E)),
                                dispatch[:, UP_TO:UP_TO + E * E].rearrange("p (a b) -> p a b", b=E), ALU.mult)
                order.then(v.scalar_tensor_tensor(out=r(RANK), in0=r(TMP), scalar=-float(P), in1=r(RANK),
                                                  op0=ALU.mult, op1=ALU.add))
                both = route[:, ONE:TWO + 1, :]
                pair = route[:, PAIR:PAIR + 2, :]

                def of_assignment(what, to):
                    order.then(v.tensor_tensor(pair, both, route[:, what, :].unsqueeze(1)
                                               .to_broadcast((P, 2, TT * E)), ALU.mult))
                    return v.tensor_reduce(to[:], pair.rearrange("p c (t e) -> p (c t) e", e=E), AX, ALU.add)

                of_assignment(RANK, slot_of)
                order.then(v.tensor_reduce(cum, sums[:], AX, ALU.add))
                order.then(v.tensor_scalar(cum, cum, float(E), None, ALU.add))
                order.then(v.scalar_tensor_tensor(out=off, in0=cum, scalar=-1.0, in1=more, op0=ALU.add,
                                                  op1=ALU.subtract))
                v.tensor_scalar(r(BLOCK), r(TMP), 1.0, None, ALU.min)
                order.then(v.tensor_tensor(off, off, const("expert"), ALU.subtract))
                v.tensor_tensor(r(TMP), r(TMP), over_t(const("expert")), ALU.add)
                order.then(v.tensor_tensor(r(BLOCK), r(BLOCK), over_t(off), ALU.mult))
                order.then(v.tensor_tensor(r(BLOCK), r(BLOCK), r(TMP), ALU.add))
                order.then(of_assignment(BLOCK, block_of))
                v.tensor_tensor(slot_hot[:], slot_of[:].unsqueeze(2).to_broadcast((P, 2 * TT, P)),
                                dispatch[:, 0:P].unsqueeze(1).to_broadcast((P, 2 * TT, P)), ALU.is_equal)
                order.then(v.tensor_tensor(block_hot[:], block_of[:].unsqueeze(2).to_broadcast((P, 2 * TT, NBLK)),
                                           const("block").unsqueeze(1).to_broadcast((P, 2 * TT, NBLK)), ALU.is_equal))
                rows = dispatch[:, P:P + 4 * TT].rearrange("p (a c) -> p a c", c=2)
                for c in range(2):
                    i = v.tensor_tensor(row_hot[:, :, c, :], block_hot[:],
                                        rows[:, :, c:c + 1].to_broadcast((P, 2 * TT, NBLK)), ALU.mult)
                i.then_inc(hot_ready, 1)
                order.then(v.tensor_tensor(over[:], cum.unsqueeze(1).to_broadcast((P, NBLK, E)),
                                           const("block").unsqueeze(2).to_broadcast((P, NBLK, E)), ALU.is_le))
                v.wait_ge(table_made, 1)
                v.tensor_scalar(slot_table[:].rearrange("p c b -> p (c b)"), ps[:, 3, 0:2 * NBLK], float(EMPTY), None,
                                ALU.add).then_inc(table_ready, 1)
                order.then(v.tensor_reduce(block_f[:, 0:NBLK], over[:], AX, ALU.add))
                order.then(v.tensor_tensor(block_f[:, 0:E], block_f[:, 0:E], const("expert"), ALU.add))
                order.then(v.tensor_scalar(block_f[:, 0:NBLK], block_f[:, 0:NBLK], float(E - 1), None, ALU.min))
                v.tensor_copy(block_f[:, NBLK:NBLK + 1], cum[:, E - 1:E])
                order.then(v.tensor_scalar(block_f[:, NBLK + 1:NBLK + 2], cum[:, E - 1:E], -1.0, None, ALU.add))
                v.tensor_copy(block_i[:], block_f[:]).then_inc(blocks_ready, 1)
                v.wait_ge(blocks_ready, 1)

            with nc.Block() as block:
                @block.sync
                def _(sp):
                    def source(x):
                        if x["kind"] == "ZT":
                            return projection_columns(layer, x["tile"], x["half"])
                        if x["kind"] == "ZN":
                            return a["w_in"][layer].rearrange("(k p) n -> p k n", p=P)[
                                :, 4 * x["half"]:4 * x["half"] + 4, x["tile"] * W:(x["tile"] + 1) * W]
                        if x["kind"] == "gate":
                            return a["w_gate"][layer, x["b"]].rearrange("(k p) n -> p k n", p=P)[
                                :, :, x["q"] * 256:x["q"] * 256 + 256]
                        if x["kind"] == "branch":
                            return a["w_branch"][layer, x["b"]].rearrange("(k p) n -> p k n", p=P)[
                                :, :, x["q"] * 256:x["q"] * 256 + 256]
                        return a["w_o"][layer].rearrange("(k p) n -> p k n", p=P)[
                            :, 4 * x["half"]:4 * x["half"] + 4, x["n"] * 512:x["n"] * 512 + 512]

                    def event(*unit):
                        return min(c_of[unit] + 6, nchunk - 1)

                    def parameters():
                        sp.dma_start(prow[0:32, :], a["b_gate"][layer].rearrange("b (m p) -> (b m) p", p=P))\
                          .then_inc(params_in, 16)
                        sp.dma_start(prow[32:44, :], a["conv_w"][layer].rearrange("k o (m p) -> (k o m) p", p=P))\
                          .then_inc(params_in, 16)
                        sp.dma_start(prow[44:45, :], a["diff_subln_g"][bass.ds(layer, 1), :]).then_inc(params_in, 16)
                        for i, name in enumerate(("lambda_q1", "lambda_q2", "lambda_k1", "lambda_k2")):
                            sp.dma_start(lam_rows[:, i, :], a[name][bass.ds(layer, 1), :].to_broadcast((P, 64)))\
                              .then_inc(params_in, 16)
                        lo = CONST["lam"][0]
                        sp.dma_start(lam_in, a["consts"][:, bass.ds(layer * 2 + lo, 2)]).then_inc(params_in, 16)

                    def rotary_tables():
                        sp.wait_ge(tables_saved, 16)
                        sp.dma_start(tables[:, 0:4, :], a["tables"][:, 0:4, :]).then_inc(tables_back, 16)
                        sp.dma_start(causal, a["causal"][:, :]).then_inc(tables_back, 16)

                    def decays(hd):
                        if hd >= 2:
                            sp.wait_ge(decayed, hd - 1)
                        sp.dma_start(decay[:, hd % 2, :], a["decay"][hd]).then_inc(decay_in[hd % 2], 16)

                    def spatial_weights():
                        sp.wait_ge(att_turned, 4 * TT)
                        sp.dma_start(att[:, 0, :].rearrange("p (g s) -> p g s", g=4),
                                     a["w_s"][layer].rearrange("g t s -> t g s")).then_inc(ws_in, 16)

                    def spatial_norm():
                        sp.wait_ge(decayed, 4)
                        sp.dma_start(decay[:, 0, :], a["sgu_ln_g"][bass.ds(layer, 1), :].to_broadcast((P, W)))\
                          .then_inc(tables_in, 16)
                        sp.dma_start(decay[:, 1, :], a["sgu_ln_b"][bass.ds(layer, 1), :].to_broadcast((P, W)))\
                          .then_inc(tables_in, 16)
                        sp.wait_ge(ret_values_ready, 4)
                        sp.dma_start(attT[:, 0, :], a["b_s"][bass.ds(layer, 1)].rearrange("a g t -> a (g t)")
                                     .to_broadcast((P, W))).then_inc(tables_in, 16)

                    def residual():
                        sp.wait_ge(y_tails, 3)
                        sp.dma_start(ln1_gb[:, 0, :], a["ln1_g"][bass.ds(layer, 1), :].to_broadcast((P, D)))\
                          .then_inc(ln1_in, 16)
                        sp.dma_start(ln1_gb[:, 1, :], a["ln1_b"][bass.ds(layer, 1), :].to_broadcast((P, D)))\
                          .then_inc(ln1_in, 16)
                        sp.wait_ge(x_saved, 16 * TT)
                        sp.wait_ge(y_tails, 4)
                        sp.dma_start(h[:], out_tiles).then_inc(h_back, 16)

                    loads = {}
                    for c, what in ((2, parameters), (4, rotary_tables), (6, lambda: decays(0)), (7, lambda: decays(1)),
                                    (event("diff_transpose", 4 * TT - 1), spatial_weights),
                                    (event("ret_scores", 0), lambda: decays(2)),
                                    (event("ret_scores", 1), lambda: decays(3)),
                                    (event("ret_values", 3), spatial_norm),
                                    (event("split", SGU), residual)):
                        loads.setdefault(c, []).append(what)
                    for c, x in list(enumerate(plan))[1:]:
                        for what in loads.get(c, []):
                            what()
                        if c >= NRAW:
                            sp.wait_ge(chunk_used, c - NRAW + 1)
                        sp.dma_start(raw_view(raw[c % NRAW], x), source(x)).then_inc(raw_in[c % NRAW], 16)

                    def expert_chunk(m, e, j, slot, count):
                        sp.wait_ge(e_tails, count)
                        sp.dma_start(e_raw[slot][:], a[m][layer, e, 256 * j:256 * j + 256, :]
                                     .rearrange("(p s) f -> p s f", s=2)).then_inc(e_raw_in[slot], 16)

                    sp.wait_ge(z_moved, z_all[SGU])
                    sp.wait_ge(y_tails, 4)
                    sp.dma_start(w_router[:], a["w_router"].rearrange("(k p) e -> p k e", p=P)).then_inc(router_in, 16)
                    sp.dma_start(b_router[:], a["b_router"].rearrange("(a e) -> a e", a=1).to_broadcast((P, E)))\
                      .then_inc(router_in, 16)
                    sp.dma_start(dispatch[:], a["dispatch"][:, :]).then_inc(router_in, 16)
                    sp.wait_ge(chunk_used, gate_chunk[SGU][-1] + 2)
                    sp.wait_ge(m_tails, 4)
                    for j in range(8):
                        if j == EARLY:
                            sp.wait_ge(out_tile, TT)
                        if j >= AHEAD:
                            sp.wait_ge(e_raw_in[j - AHEAD], 16)
                        expert_chunk(("w1", "w3")[j // 4], 0, j % 4, j, j + 1)
                    n = None
                    prev = 0
                    for i in (1, None):
                        def body(i, prev, e, first):
                            for j in range(12):
                                slot = (8 + j) % 12
                                count = 12 * i - 4 + j + 1
                                if first:
                                    if slot >= AHEAD and j < 4:
                                        sp.wait_ge(e_raw_in[slot - AHEAD], 16)
                                    if slot == NER - 2:
                                        sp.wait_ge(logits_ready, 1)
                                else:
                                    count = sp.snap(count)
                                    before = sp.snap(16 * i + (16 if j - AHEAD >= 4 else 0))
                                    sp.wait_ge(e_raw_in[(8 + j - AHEAD) % 12], before)
                                    sp.sem_inc(queue_short, 1)
                                m, ee = (("w1", e), ("w3", e), ("w2", prev))[j // 4]
                                expert_chunk(m, ee, j % 4, slot, count)
                        if i == 1:
                            body(1, 0, 1, True)
                            sp.wait_ge(blocks_ready, 1)
                            n = sp.value_load(block_i[0:1, NBLK:NBLK + 1], min_val=E, max_val=E + OVF)
                        else:
                            with sp.Fori(2, n) as i:
                                e = sp.value_load(block_i[0:1, bass.ds(i, 1)], min_val=0, max_val=E - 1)
                                prev = sp.value_load(block_i[0:1, bass.ds(i - 1, 1)], min_val=0, max_val=E - 1)
                                body(i, prev, e, False)
                    last = sp.value_load(block_i[0:1, NBLK + 1:NBLK + 2], min_val=E - 1, max_val=E + OVF - 1)
                    e = sp.value_load(block_i[0:1, bass.ds(last, 1)], min_val=0, max_val=E - 1)
                    for j in range(4):
                        count = sp.snap(12 * last + 8 + j + 1)
                        expert_chunk("w2", e, j, (8 + j) % 12, count)
                    x_split = sp.snap(4 * last + 4)
                    sp.wait_ge(e_t_tails, x_split)
                    for i, name in enumerate(("ln2_g", "ln2_b")):
                        sp.dma_start(ln2_gb[:, i, :], a[name][bass.ds(layer, 1), :].to_broadcast((P, D)))\
                          .then_inc(ln2_in, 16)
                    next_layer = sp.snap((layer + 1) % DEPTH)
                    count = sp.snap(12 * last + 20)
                    sp.wait_ge(e_tails, count)
                    start2.sync(sp, projection_columns(next_layer, plan[0]["tile"], plan[0]["half"]))
                    sp.wait_ge(ln2_in, 32)
                    sp.wait_ge(start2.landed, 16)

                @block.gpsimd
                def _(pool):
                    def tail(c):
                        x = plan[c]
                        pool.wait_ge(heads, c + 1)
                        pool.tensor_tensor(raw_view(w_tail[c % NRAW], x), raw_view(raw[c % NRAW], x),
                                           raw_view(w_head[c % NHEAD], x), ALU.subtract).then_inc(tails, 1)

                    pool.sem_inc(tails, 1)
                    for c in range(1, nchunk):
                        tail(c)
                    pool.wait_ge(ln1_in, 32)
                    norm1.gpsimd(pool, ln1_gb[:, 1, :])
                    pool.memset(x_rows[:], 0.0).then_inc(x_cleared, 1)
                    pool.wait_ge(table_ready, 1)
                    pool.wait_ge(x_cleared, 1)
                    pool.sem_inc(out_free, 1)

                    def indices(i, which, to, count, also, by):
                        pool.tensor_copy(to[:], slot_table[:, which:which + 1, bass.ds(i, 1)]
                                         .rearrange("p a b -> p (a b)")).then_inc(index_ready, 1)
                        pool.wait_ge(also, by)
                        pool.wait_ge(index_ready, count)
                        pool.sem_inc(index_seen, 1)

                    def load_x(i, count):
                        indices(i, 0, x_index, count, h1_saved, 16 * TT)
                        pool.indirect_dma_start(x_rows[:], None, h1_rows[:, :], bass.IndirectOffsetOnAxis(x_index[:], 0),
                                                bounds_check=T - 1, oob_is_err=False).then_inc(x_in, 16)

                    def store_y(i, count, moved, stored):
                        indices(i, 1, y_index, count, out_moved, moved)
                        pool.indirect_dma_start(y_rows[:, :], bass.IndirectOffsetOnAxis(y_index[:], 0), e_out[:], None,
                                                bounds_check=2 * T - 1, oob_is_err=False).then_inc(y_stored, 16)
                        pool.wait_ge(y_stored, stored)
                        pool.sem_inc(out_free, 1)

                    load_x(0, 1)
                    pool.wait_ge(e_turned, 2)
                    load_x(1, 2)
                    pool.wait_ge(e_turned, 4)
                    load_x(2, 3)
                    pool.wait_ge(blocks_ready, 1)
                    n = pool.value_load(block_i[0:1, NBLK:NBLK + 1], min_val=E, max_val=E + OVF)
                    with pool.Fori(2, n) as i:
                        pool.wait_ge(e_turned, 4 * i)
                        load_x(i + 1, 2 * i)
                        store_y(i - 2, 2 * i + 1, i, 16 * i - 16)
                    last = pool.value_load(block_i[0:1, NBLK + 1:NBLK + 2], min_val=E - 1, max_val=E + OVF - 1)
                    for d in (0, 1):
                        store_y(last - 1 + d, 2 * last + 2 + d, last + 1 + d, 16 * last + 16 * d)
                    pool.wait_ge(x_in, 16 * last + 32)

                @block.scalar
                def _(act):
                    def head(c):
                        x = plan[c]
                        act.wait_ge(raw_in[c % NRAW], 16 * (c // NRAW + (1 if c % NRAW else 0)))
                        if c >= NHEAD:
                            act.wait_ge(chunk_used, c - NHEAD + 1)
                        act.activation(raw_view(w_head[c % NHEAD], x), raw_view(raw[c % NRAW], x), ACT.Copy)\
                           .then_inc(heads, 1)

                    def unit(kind, *g):
                        if kind == "split":
                            b = g[0]
                            i = ORDER.index(b)
                            act.wait_ge(*y_done[b])
                            if i:
                                act.wait_ge(chunk_used, gate_chunk[ORDER[i - 1]][-1] + 2)
                            act.activation(yT_head[:], y_of[b], ACT.Copy).then_inc(y_heads, 1)
                        elif kind == "diff_scores":
                            u, w = g[0], P * (g[0] % TT + 1)
                            act.wait_ge(masked, u + 1)
                            for c in range(2):
                                i = act.activation(att[:, c, 0:w], att[:, c, 0:w], ACT.Exp, bias=top[:, c:c + 1],
                                                   scale=0.125, accum_out=rowsum[:, c:c + 1])
                            i.then_inc(exps_done, 1)
                        elif kind == "diff_transpose":
                            u, it = g[0], g[0] % TT
                            act.wait_ge(att_turned, u + 1)
                            if u >= TT:
                                act.wait_ge(values_ready, u // TT)
                            act.activation(attT[:, 0:it + 1, it * P:(it + 1) * P],
                                           ps[:, 6, 0:(it + 1) * P].rearrange("p (j i) -> p j i", i=P), ACT.Copy)\
                               .then_inc(att_copied, 1)
                        elif kind in ("diff_values", "ret_values"):
                            n = g[0] + (4 if kind == "ret_values" else 0)
                            act.wait_ge(ret_values_ready if n >= 4 else values_ready, g[0] + 1)
                            if n:
                                act.wait_ge(summed, n)
                            act.activation(square[:], ps[:, 4 if n >= 4 else 7, :], ACT.Square).then_inc(squared, 1)
                            if n >= 4:
                                act.wait_ge(normed, n)
                                act.activation(silu[:], z1[:, 2, g[0], :], ACT.Sigmoid).then_inc(silu_ready, 1)
                        elif kind in ("diff_norm", "ret_norm"):
                            n = g[0] + (4 if kind == "ret_norm" else 0)
                            act.wait_ge(summed, n + 1)
                            if n:
                                act.wait_ge(normed, n)
                            act.activation(std[:], ps[:, 5 if n >= 4 else 6, :], ACT.Sqrt, scale=1.0 / 128,
                                           bias=const("eps")[:, 1:2]).then_inc(rooted, 1)
                        elif kind == "sgu_norm":
                            n = g[0]
                            act.wait_ge(var_ready, n + 1)
                            act.activation(ln_sd[:, n:n + 1], ln_mv[:, n, 1:2], ACT.Sqrt, bias=const("eps")[:, 0:1])\
                               .then_inc(sgu_root, 1)
                        elif kind == "merge_split":
                            q = g[0]
                            act.wait_ge(chunk_used, gate_chunk[SGU][-1] + 1)
                            act.wait_ge(merged_done, 4 * 3 + q + 1)
                            act.activation(hT_head[:, 2 * q:2 * q + 2, :], merged[:, 2 * q:2 * q + 2, :], ACT.Copy)\
                               .then_inc(m_heads, 1)

                    act.sem_inc(heads, 1)
                    for c in range(1, NHEAD):
                        head(c)

                    def tile_of(x, t):
                        return x[:, :, t * P:(t + 1) * P]

                    def turned_tile(t):
                        return ps[:, 2 * t:2 * t + 2, :].rearrange("p a (k i) -> p (a k) i", i=P)

                    for c, x in enumerate(plan):
                        for unit_ in x["mid"]:
                            unit(*unit_)
                        banks = slice(2 * (c % 2), 2 * (c % 2) + 2)
                        if x["kind"] in ("ZT", "ZN") and not (x["kind"] == "ZN" and not x["half"]):
                            act.wait_ge(chunk_used, c + 1)
                            if x["b"] == RET:
                                act.wait_ge(y_tails, 1)
                            if x["b"] == SGU:
                                act.wait_ge(y_tails, 2)
                            if x["kind"] == "ZT":
                                act.activation(z[ZBUF[x["b"]]][:, x["g"], 2 * x["half"]:2 * x["half"] + 2, :],
                                               ps[:, banks, :], ACT.Copy).then_inc(z_moved, 1)
                            else:
                                act.activation(z[ZBUF[x["b"]]][:, x["g"], :, :], ps[:, 0:4, :], ACT.Copy)\
                                   .then_inc(z_moved, 1)
                        if x["kind"] == "gate":
                            n = free_by[c][1]
                            act.wait_ge(chunk_used, c + 1)
                            if n > 1:
                                act.wait_ge(merged_done, n - 1)
                            else:
                                act.wait_ge(prm_ready, 1)
                            for m in range(2):
                                bias = prm[:, x["b"] * 8 + 2 * x["q"] + m:x["b"] * 8 + 2 * x["q"] + m + 1]
                                i = act.activation(gate[:, m, :], ps[:, 2 * (c % 2) + m, :], ACT.Sigmoid, bias=bias)
                            i.then_inc(gates_done, 1)
                        if c + NHEAD < nchunk:
                            head(c + NHEAD)
                        if c == 1:
                            act.wait_ge(lam_exp_in, 1)
                            act.activation(lam[:, 0:2], lam[:, 2:4], ACT.Exp).then_inc(lam_exp, 1)
                        for unit_ in x["units"]:
                            unit(*unit_)
                    norm1.scalar(act, const("eps")[:, 0:1])

                    def copy_logits(t):
                        act.wait_ge(logits_made, t + 1)
                        act.activation(logits_T[:, t * P:(t + 1) * P], ps[0:E, 2 * t, 0:P], ACT.Copy)\
                           .then_inc(logits_copied, 1)

                    for t in range(TT):
                        act.wait_ge(norm1.ready, t + 1)
                        act.dma_start(h1_rows[t * P:(t + 1) * P, :], h[:, t, :]).then_inc(h1_saved, 16)
                        act.wait_ge(r_turned, t + 1)
                        act.activation(tile_of(hT, t), turned_tile(t), ACT.Copy).then_inc(r_copied, 1)
                        if t:
                            copy_logits(t - 1)
                    copy_logits(TT - 1)
                    act.wait_ge(r_shift, 1)
                    act.activation(r(SCORE), r(LOGIT), ACT.Exp).then_inc(r_exp, 1)

                    act.sem_inc(out_moved, 1)

                    def e_split(slot, ring, landed, used):
                        act.wait_ge(e_raw_in[slot], landed)
                        act.wait_ge(e_used, used)
                        act.activation(e_head[ring][:], e_raw[slot][:], ACT.Copy).then_inc(e_heads, 1)

                    def e_turn(count, bank, to):
                        act.wait_ge(e_turned, count)
                        act.activation(to, ps[:, bank, :].rearrange("p (k s) -> p k s", s=P), ACT.Copy)\
                           .then_inc(e_t_heads, 1)

                    def sigmoid(i, used):
                        act.wait_ge(e_used, used)
                        if not isinstance(i, int) or i:
                            act.wait_ge(gated, i)
                        act.activation(e_sig[:], ps[:, 0:2, :], ACT.Sigmoid).then_inc(sig_done, 1)

                    def out_rows(used, free):
                        act.wait_ge(e_used, used)
                        act.wait_ge(out_free, free)
                        act.activation(e_out[:], ps[:, 4:6, :].rearrange("p a b -> p (a b)"), ACT.Copy)\
                           .then_inc(out_moved, 1)

                    def body(i, first):
                        base = 12 * i - 4

                        def head(j):
                            slot = (8 + j) % NER
                            e_split(slot, (8 + j) % NEH, 16 * i + (16 if slot < 8 else 0), base + j + 1)

                        for j in range(12):
                            head(j)
                            if j == 0 and first:
                                e_turn(3, 6, xT_head[:, 0:4, :])
                                e_turn(4, 7, xT_head[:, 4:8, :])
                            if j == 2 and not first:
                                out_rows(base + NEH, i - 1)
                            if j == 3:
                                e_turn(4 * i + 1, 6, aT_head[:, 0:4, :])
                            if j == 4:
                                e_turn(4 * i + 2, 7, aT_head[:, 4:8, :])
                            if j == 10:
                                sigmoid(i, base + 8 + NEH)
                        e_turn(4 * i + 3, 6, xT_head[:, 0:4, :])
                        e_turn(4 * i + 4, 7, xT_head[:, 4:8, :])

                    e_split(0, 0, 16, 1)
                    e_split(1, 1, 16, 2)
                    e_split(2, 2, 16, 3)
                    e_turn(1, 6, xT_head[:, 0:4, :])
                    e_turn(2, 7, xT_head[:, 4:8, :])
                    for j in range(3, 8):
                        e_split(j, j % NEH, 16, j + 1)
                        if j == 6:
                            sigmoid(0, 4 + NEH)
                    body(1, True)
                    act.wait_ge(blocks_ready, 1)
                    n = act.value_load(block_i[0:1, NBLK:NBLK + 1], min_val=E, max_val=E + OVF)
                    with act.Fori(2, n) as i:
                        body(i, False)
                    last = act.value_load(block_i[0:1, NBLK + 1:NBLK + 2], min_val=E - 1, max_val=E + OVF - 1)
                    for j in range(4):
                        slot = (8 + j) % NER
                        e_split(slot, (8 + j) % NEH, 16 * last + (32 if slot < 8 else 16), 12 * last + 8 + j + 1)
                        if j == 1:
                            e_turn(4 * last + 5, 6, aT_head[:, 0:4, :])
                            e_turn(4 * last + 6, 7, aT_head[:, 4:8, :])
                        if j == 2:
                            out_rows(12 * last + 8 + NEH, last)
                    out_rows(12 * last + 12 + NEH, last + 1)

                @block.vector
                def _(v):
                    order = Steps(v, denssig_times)
                    v.sem_inc(e_tails, NER)

                    def unit(kind, *g):
                        if kind == "split":
                            v.wait_ge(y_heads, ORDER.index(g[0]) + 1)
                            v.tensor_tensor(yT_tail[:], y_of[g[0]], yT_head[:], ALU.subtract).then_inc(y_tails, 1)
                        elif kind == "conv":
                            m = g[0]
                            if m == 0:
                                v.wait_ge(z_moved, z_all[CONV])
                            bg, cg, ug = z1[:, 0, m, :], z1[:, 1, m, :], z1[:, 2, m, :]

                            def tap(k):
                                return prm[:, 32 + 4 * k + m:33 + 4 * k + m]

                            order.then(v.tensor_tensor(cg, cg, ug, ALU.mult))
                            order.then(v.tensor_scalar(ug, cg, tap(2), None, ALU.mult))
                            for s in (1, 2):
                                order.then(v.scalar_tensor_tensor(out=ug[:, s:T], in0=cg[:, 0:T - s], scalar=tap(2 - s),
                                                                  in1=ug[:, s:T], op0=ALU.mult, op1=ALU.add))
                            v.tensor_tensor(ug, ug, bg, ALU.mult).then_inc(conv_done, 1)
                        elif kind == "rotate":
                            b, grp = g
                            n = 3 if b == RET else grp + 1
                            co, si = (cos_ret, sin_ret) if b == RET else (cos_diff, sin_diff)
                            v.wait_ge(tables_back, 32)
                            x = z[ZBUF[b]][:, grp]
                            cob, sib = (s.unsqueeze(1).to_broadcast((P, 4, T)) for s in (co, si))
                            v.wait_ge(swapped, n)
                            order.then(v.tensor_tensor(x, x, cob, ALU.mult))
                            order.then(v.tensor_tensor(attT[:], ps[:, 4:8, :], sib, ALU.mult))
                            v.tensor_tensor(x, x, attT[:], ALU.add).then_inc(rotated, 1)
                            v.wait_ge(rotated, n)
                        elif kind == "diff_scores":
                            u, it = g[0], g[0] % TT
                            w = P * (it + 1)
                            v.wait_ge(scores_ready, u + 1)
                            if u:
                                v.wait_ge(att_turned, u)
                            m = causal[:, T - w:T].unsqueeze(1).to_broadcast((P, 2, w))
                            order.then(v.tensor_tensor(att[:, :, 0:w], ps[:, 4:6, 0:w], m, ALU.add))
                            order.then(v.tensor_reduce(top, att[:, :, 0:w], AX, ALU.max))
                            v.tensor_scalar(top, top, -0.125, None, ALU.mult).then_inc(masked, 1)
                            v.wait_ge(exps_done, u + 1)
                            order.then(v.reciprocal(rowsum, rowsum))
                            order.then(v.tensor_tensor(rowsum[:, 1:2], rowsum[:, 1:2], lam[:, 2:3], ALU.mult))
                            order.then(v.tensor_scalar(att[:, 0, 0:w], att[:, 0, 0:w], rowsum[:, 0:1], None, ALU.mult))
                            v.scalar_tensor_tensor(out=att[:, 0, 0:w], in0=att[:, 1, 0:w], scalar=rowsum[:, 1:2],
                                                   in1=att[:, 0, 0:w], op0=ALU.mult, op1=ALU.add).then_inc(att_ready, 1)
                        elif kind == "diff_norm":
                            hd = g[0]
                            v.wait_ge(rooted, hd + 1)
                            order.then(v.reciprocal(std[:], std[:]))
                            v.scalar_tensor_tensor(out=z0[:, 0, hd, :], in0=ps[:, 7, :], scalar=lam[:, 3:4], in1=std[:],
                                                   op0=ALU.mult, op1=ALU.mult).then_inc(normed, 1)
                        elif kind == "ret_scores":
                            hd = g[0]
                            v.wait_ge(ret_scores_ready, hd + 1)
                            v.wait_ge(decay_in[hd % 2], 16 * (hd // 2 + 1))
                            if hd:
                                v.wait_ge(ret_values_ready, hd)
                            for jt in range(TT):
                                w = T - jt * P
                                i = v.tensor_tensor(attT[:, jt, 0:w], ps[:, 4 + jt, 0:w], decay[:, hd % 2, 0:w], ALU.mult)
                            i.then_inc(decayed, 1)
                        elif kind == "ret_norm":
                            hd = g[0]
                            v.wait_ge(silu_ready, hd + 1)
                            order.then(v.tensor_tensor(silu[:], silu[:], z1[:, 2, hd, :], ALU.mult))
                            v.wait_ge(rooted, 4 + hd + 1)
                            order.then(v.reciprocal(std[:], std[:]))
                            order.then(v.tensor_tensor(silu[:], silu[:], std[:], ALU.mult))
                            v.tensor_tensor(z1[:, 2, hd, :], ps[:, 4, :], silu[:], ALU.mult).then_inc(normed, 1)
                        elif kind == "sgu_mask":
                            v.wait_ge(ws_turned, 1)
                            v.tensor_tensor(att[:, 1, :].rearrange("p (g s) -> p g s", g=4),
                                            ps[:, 4, :].rearrange("p (g s) -> p g s", g=4),
                                            const("upper").unsqueeze(1).to_broadcast((P, 4, P)), ALU.mult)\
                             .then_inc(ws_masked, 1)
                        elif kind == "sgu_norm":
                            n = g[0]
                            x = z0[:, 1, n, :]
                            if n == 0:
                                v.wait_ge(z_moved, z_all[SGU])
                                v.wait_ge(tables_in, 48)
                            order.then(v.bn_stats(ln_stats[:, n, 0, :], x))
                            v.bn_aggr(ln_mv[:, n, :], ln_stats[:, n, 0, :]).then_inc(var_ready, 1)
                            v.wait_ge(sgu_root, n + 1)
                            order.then(v.reciprocal(ln_sd[:, n:n + 1], ln_sd[:, n:n + 1]))
                            order.then(v.tensor_scalar(x, x, ln_mv[:, n, 0:1], ln_sd[:, n:n + 1], ALU.subtract, ALU.mult))
                            order.then(v.tensor_tensor(x, x, decay[:, 0, :], ALU.mult))
                            v.tensor_tensor(x, x, decay[:, 1, :], ALU.add).then_inc(sgu_normed, 1)
                        elif kind == "sgu_mix":
                            v.wait_ge(mixed_ready, 1)
                            s4 = z0[:, 1].rearrange("p g (n t) -> p g n t", t=P)
                            for grp in range(4):
                                i = v.tensor_tensor(s4[:, grp], ps[:, 4 + grp, :].rearrange("p (n t) -> p n t", t=P),
                                                    attT[:, 0, grp * P:(grp + 1) * P].unsqueeze(1).to_broadcast((P, 4, P)),
                                                    ALU.add)
                            order.then(i)
                            v.tensor_tensor(z0[:, 0], z0[:, 0], z0[:, 1], ALU.mult).then_inc(sgu_done, 1)
                        elif kind == "merge_split":
                            q = g[0]
                            v.wait_ge(m_heads, q + 1)
                            v.tensor_tensor(hT_tail[:, 2 * q:2 * q + 2, :], merged[:, 2 * q:2 * q + 2, :],
                                            hT_head[:, 2 * q:2 * q + 2, :], ALU.subtract).then_inc(m_tails, 1)

                    v.wait_ge(prm_turned, 1)
                    v.tensor_copy(prm[:], ps[:, 4, 0:45]).then_inc(prm_ready, 1)
                    v.wait_ge(prm_ready, 1)
                    order.then(v.tensor_tensor(lam_rows[:, 0:2, :], lam_rows[:, 0:2, :], lam_rows[:, 2:4, :], ALU.mult))
                    v.tensor_reduce(lam[:, 2:4], lam_rows[:, 0:2, :], AX, ALU.add).then_inc(lam_exp_in, 1)
                    v.wait_ge(lam_exp, 1)
                    order.then(v.tensor_tensor(lam[:, 2:3], lam[:, 1:2], lam[:, 0:1], ALU.subtract))
                    order.then(v.tensor_tensor(lam[:, 2:3], lam[:, 2:3], lam_in[:, 0:1], ALU.subtract))
                    order.then(v.tensor_tensor(lam[:, 3:4], prm[:, 44:45], lam_in[:, 1:2], ALU.mult))
                    for c, x in enumerate(plan):
                        for unit_ in x["mid"]:
                            unit(*unit_)
                        if x["kind"] == "branch":
                            n = free_by[c][1]
                            q = x["q"]
                            bank = 2 * (c % 2)
                            v.wait_ge(chunk_used, c + 1)
                            v.wait_ge(gates_done, n)
                            m2 = merged[:, 2 * q:2 * q + 2, :]
                            if x["b"] == ORDER[0]:
                                v.tensor_tensor(m2, ps[:, bank:bank + 2, :], gate[:], ALU.mult).then_inc(merged_done, 1)
                            else:
                                order.then(v.tensor_tensor(gate[:], ps[:, bank:bank + 2, :], gate[:], ALU.mult))
                                v.tensor_tensor(m2, m2, gate[:], ALU.add).then_inc(merged_done, 1)
                        if x["kind"] == "wo" and x["half"] and x["n"] == 0:
                            v.wait_ge(chunk_used, c + 1)
                            v.wait_ge(h_back, 16)
                            hn = h[:, :, 0:512]
                            v.scalar_tensor_tensor(out=hn, in0=hn, scalar=ALPHA, in1=ps[:, 0:4, :], op0=ALU.mult,
                                                   op1=ALU.add).then_inc(summed_out, 1)
                        for unit_ in x["units"]:
                            unit(*unit_)
                    v.wait_ge(ln1_in, 32)
                    v.wait_ge(summed_out, 1)

                    def add_residual(v, order, t):
                        v.wait_ge(out_tile, t + 1)
                        order.then(v.scalar_tensor_tensor(out=h[:, t, 512:1024], in0=h[:, t, 512:1024], scalar=ALPHA,
                                                          in1=ps[:, 4 + t, :], op0=ALU.mult, op1=ALU.add))

                    norm1.vector(v, order, add_residual, ln1_gb[:, 0, :])
                    router(v, order)

                    def e_split(slot, ring, count):
                        v.wait_ge(e_heads, count)
                        v.tensor_tensor(e_tail[ring][:], e_raw[slot][:], e_head[ring][:], ALU.subtract)\
                         .then_inc(e_tails, 1)

                    def e_turn(count, bank, head_, to):
                        v.wait_ge(e_t_heads, count)
                        v.tensor_tensor(to, ps[:, bank, :].rearrange("p (k s) -> p k s", s=P), head_, ALU.subtract)\
                         .then_inc(e_t_tails, 1)

                    def sigmoid_times(i):
                        v.wait_ge(sig_done, i + 1)
                        v.tensor_tensor(act_rows[:], ps[:, 0:2, :], e_sig[:], ALU.mult).then_inc(sig_times, 1)

                    def gated_rows(i, used):
                        v.wait_ge(e_used, used)
                        v.wait_ge(sig_times, i + 1)
                        v.tensor_tensor(act_rows[:], ps[:, 2:4, :], act_rows[:], ALU.mult).then_inc(gated, 1)

                    def body(i, first=False):
                        base = 12 * i - 4
                        for j in range(12):
                            e_split((8 + j) % NER, (8 + j) % NEH, base + j + 1)
                            if j == 0 and first:
                                gated_rows(0, 8 + NEH)
                                e_turn(3, 6, xT_head[:, 0:4, :], xT_tail[:, 0:4, :])
                                e_turn(4, 7, xT_head[:, 4:8, :], xT_tail[:, 4:8, :])
                            if j == 3:
                                e_turn(4 * i + 1, 6, aT_head[:, 0:4, :], aT_tail[:, 0:4, :])
                            if j == 4:
                                e_turn(4 * i + 2, 7, aT_head[:, 4:8, :], aT_tail[:, 4:8, :])
                            if j == 10:
                                sigmoid_times(i)
                                gated_rows(i, base + 8 + NEH)
                        e_turn(4 * i + 3, 6, xT_head[:, 0:4, :], xT_tail[:, 0:4, :])
                        e_turn(4 * i + 4, 7, xT_head[:, 4:8, :], xT_tail[:, 4:8, :])

                    for j in range(3):
                        e_split(j, j, j + 1)
                    e_turn(1, 6, xT_head[:, 0:4, :], xT_tail[:, 0:4, :])
                    e_turn(2, 7, xT_head[:, 4:8, :], xT_tail[:, 4:8, :])
                    for j in range(3, 8):
                        e_split(j, j % NEH, j + 1)
                        if j == 7:
                            sigmoid_times(0)
                    body(1, True)
                    n = v.value_load(block_i[0:1, NBLK:NBLK + 1], min_val=E, max_val=E + OVF)
                    with v.Fori(2, n) as i:
                        body(i)
                    last = v.value_load(block_i[0:1, NBLK + 1:NBLK + 2], min_val=E - 1, max_val=E + OVF - 1)
                    for j in range(4):
                        e_split((8 + j) % NER, (8 + j) % NEH, 12 * last + 8 + j + 1)
                        if j == 1:
                            e_turn(4 * last + 5, 6, aT_head[:, 0:4, :], aT_tail[:, 0:4, :])
                            e_turn(4 * last + 6, 7, aT_head[:, 4:8, :], aT_tail[:, 4:8, :])

                @block.tensor
                def _(pe):
                    ident = const("ident")

                    def pair_of(c, x, half):
                        return half if wide_bank(x) or (c - x["half"]) % 2 == 0 else 1 - half

                    def banks_free(c, x, half):
                        if is_narrow(x):
                            if c >= 2 and half == 0:
                                pe.wait_ge(*free_by[c - 2])
                        elif x["half"] == 0 and wide_bank(x):
                            pe.wait_ge(sgu_done, 1)
                        elif x["half"] == 0:
                            pe.wait_ge(*free_by[c - 2 + half])

                    def products(c, x, half):
                        wh, wt = raw_view(w_head[c % NHEAD], x), raw_view(w_tail[c % NRAW], x)
                        if is_narrow(x):
                            nk, (xh, xt) = (4, (yT_head, yT_tail)) if x["kind"] == "branch" else (8, (hT_head, hT_tail))
                            m = half
                            o = ps[:, 2 * (c % 2) + m, :]
                            for k in range(nk):
                                lh, lt = wh[:, k, m * P:(m + 1) * P], wt[:, k, m * P:(m + 1) * P]
                                nc.tensor.matmul(o, lh, xh[:, k, :], start=k == 0, stop=False)
                                nc.tensor.matmul(o, lh, xt[:, k, :], start=False, stop=False)
                                i = nc.tensor.matmul(o, lt, xh[:, k, :], start=False, stop=k == nk - 1)
                        else:
                            k0 = 4 * x["half"]
                            pair = pair_of(c, x, half)
                            for m in (2 * pair, 2 * pair + 1):
                                o = ps[:, wide_bank(x) + m, :]
                                for k in range(4):
                                    lh = hT_head[:, k0 + k, m * P:(m + 1) * P]
                                    lt = hT_tail[:, k0 + k, m * P:(m + 1) * P]
                                    nc.tensor.matmul(o, lh, wh[:, k, :], start=x["half"] == 0 and k == 0, stop=False)
                                    nc.tensor.matmul(o, lh, wt[:, k, :], start=False, stop=False)
                                    i = nc.tensor.matmul(o, lt, wh[:, k, :], start=False,
                                                         stop=x["half"] == 1 and k == 3)
                                if c == nchunk - 1:
                                    i.then_inc(out_tile, 1)
                        return i

                    def unit(kind, *g):
                        if kind == "rotate":
                            b, grp = g
                            n = 3 if b == RET else grp + 1
                            if b == RET:
                                pe.wait_ge(z_moved, z_count[(RET, 0, 1)])
                                pe.wait_ge(normed, 4)
                                pe.wait_ge(att_copied, 4 * TT)
                            else:
                                pe.wait_ge(z_moved, z_count[(DIFF, grp, 1)])
                                if n > 1:
                                    pe.wait_ge(rotated, n - 1)
                                else:
                                    pe.wait_ge(prm_ready, 1)
                            for m in range(4):
                                i = nc.tensor.matmul(ps[:, 4 + m, :], const("swap_ret" if b == RET else "swap_diff"),
                                                     z[ZBUF[b]][:, grp, m, :], start=True, stop=True)
                            i.then_inc(swapped, 1)
                        elif kind == "diff_scores":
                            u, hd, it = g[0], g[0] // TT, g[0] % TT
                            w = P * (it + 1)
                            if u:
                                pe.wait_ge(masked, u)
                            else:
                                pe.wait_ge(rotated, 2)
                            for c in range(2):
                                rows = slice(64 * c, 64 * c + 64)
                                i = nc.tensor.matmul(ps[:, 4 + c, 0:w], z0[rows, 0, hd, it * P:(it + 1) * P],
                                                     z0[rows, 1, hd, 0:w], start=True, stop=True)
                            i.then_inc(scores_ready, 1)
                        elif kind == "diff_transpose":
                            u, it = g[0], g[0] % TT
                            pe.wait_ge(att_ready, u + 1)
                            if u:
                                pe.wait_ge(att_copied, u)
                            done = [hd for hd in range(4) if turned_before_norm[hd] <= u]
                            if done:
                                pe.wait_ge(rooted, len(done))
                            for j in range(it + 1):
                                i = nc.tensor.transpose(ps[:, 6, j * P:(j + 1) * P], att[:, 0, j * P:(j + 1) * P], ident)
                            i.then_inc(att_turned, 1)
                        elif kind == "diff_values":
                            hd = g[0]
                            pe.wait_ge(att_copied, TT * (hd + 1))
                            if hd == 0:
                                pe.wait_ge(z_moved, z_all[DIFF])
                            else:
                                pe.wait_ge(normed, hd)
                            for j in range(TT):
                                i = nc.tensor.matmul(ps[:, 7, j * P:T], z0[:, 2, j, hd * P:(hd + 1) * P],
                                                     attT[:, j, j * P:T], start=j == 0, stop=j == TT - 1)
                            i.then_inc(values_ready, 1)
                        elif kind == "diff_norm":
                            hd = g[0]
                            pe.wait_ge(squared, hd + 1)
                            pe.wait_ge(att_copied, turned_before_norm[hd])
                            nc.tensor.matmul(ps[:, 6, :], const("ones"), square[:], start=True, stop=True)\
                              .then_inc(summed, 1)
                        elif kind == "ret_scores":
                            hd = g[0]
                            r, m = slice(64 * (hd % 2), 64 * (hd % 2) + 64), hd // 2
                            if hd == 0:
                                pe.wait_ge(rotated, 3)
                            else:
                                pe.wait_ge(normed, 4 + hd)
                            for j in range(TT):
                                i = nc.tensor.matmul(ps[:, 4 + j, 0:T - j * P], z1[r, 0, 2 + m, j * P:(j + 1) * P],
                                                     z1[r, 0, m, j * P:T], start=True, stop=True)
                            i.then_inc(ret_scores_ready, 1)
                        elif kind == "ret_values":
                            hd = g[0]
                            if hd == 0:
                                pe.wait_ge(z_moved, z_all[RET])
                            pe.wait_ge(decayed, hd + 1)
                            for j in range(TT):
                                i = nc.tensor.matmul(ps[:, 4, j * P:T], z1[:, 1, j, hd * P:(hd + 1) * P],
                                                     attT[:, j, 0:T - j * P], start=j == 0, stop=j == TT - 1)
                            i.then_inc(ret_values_ready, 1)
                        elif kind == "ret_norm":
                            pe.wait_ge(squared, 4 + g[0] + 1)
                            nc.tensor.matmul(ps[:, 5, :], const("ones"), square[:], start=True, stop=True)\
                              .then_inc(summed, 1)
                        elif kind == "sgu_mask":
                            pe.wait_ge(ws_in, 16)
                            pe.wait_ge(normed, 8)
                            for grp in range(4):
                                i = nc.tensor.transpose(ps[:, 4, grp * P:(grp + 1) * P], att[:, 0, grp * P:(grp + 1) * P],
                                                        ident)
                            i.then_inc(ws_turned, 1)
                        elif kind == "sgu_mix":
                            pe.wait_ge(ws_masked, 1)
                            pe.wait_ge(sgu_normed, TT)
                            for grp in range(4):
                                for n in range(TT):
                                    i = nc.tensor.matmul(ps[:, 4 + grp, n * P:(n + 1) * P],
                                                         z0[:, 1, n, grp * P:(grp + 1) * P],
                                                         att[:, 1, grp * P:(grp + 1) * P], start=True, stop=True)
                            i.then_inc(mixed_ready, 1)

                    def turn_tile(t, done):
                        for k in range(KD):
                            i = nc.tensor.transpose(ps[:, 2 * t + k // 4, (k % 4) * P:(k % 4 + 1) * P],
                                                    h[:, t, k * P:(k + 1) * P], ident)
                        i.then_inc(done, 1)

                    for c, x in enumerate(plan):
                        pe.wait_ge(tails, c + 1)
                        banks_free(c, x, 0)
                        if x["kind"] == "branch":
                            pe.wait_ge(y_tails, ORDER.index(x["b"]) + 1)
                        if x["kind"] == "wo":
                            pe.wait_ge(m_tails, 2 * x["half"] + 2)
                        products(c, x, 0)
                        for unit_ in x["mid"]:
                            unit(*unit_)
                        banks_free(c, x, 1)
                        last = products(c, x, 1)
                        if c < nchunk - 1:
                            last.then_inc(chunk_used, 1)
                        for unit_ in x["units"]:
                            unit(*unit_)
                        if c == 1:
                            pe.wait_ge(params_in, 128)
                            nc.tensor.transpose(ps[:, 4, 0:45], prow[:], ident[0:45, 0:45]).then_inc(prm_turned, 1)

                    pe.wait_ge(router_in, 48)
                    def logits(t):
                        pe.wait_ge(r_copied, t + 1)
                        for k in range(KD):
                            i = nc.tensor.matmul(ps[0:E, 2 * t, 0:P], w_router[:, k, :],
                                                 hT[:, k, t * P:(t + 1) * P], start=k == 0, stop=k == KD - 1)
                        i.then_inc(logits_made, 1)

                    for t in range(TT):
                        pe.wait_ge(norm1.ready, t + 1)
                        turn_tile(t, r_turned)
                        if t:
                            logits(t - 1)
                    logits(TT - 1)
                    for t in range(TT):
                        pe.wait_ge(logits_copied, t + 1)
                        i = nc.tensor.transpose(ps[:, 1, t * E:(t + 1) * E], logits_T[:, t * P:(t + 1) * P],
                                                ident[0:E, 0:E])
                    i.then_inc(logits_ready, 1)
                    pe.wait_ge(chosen, 1)
                    for bank, of in ((1, "strict"), (2, "ones")):
                        i = nc.tensor.matmul(ps[:, bank, 0:TT * E], const(of), route[:, BOTH, :], start=True, stop=True)
                    i.then_inc(counted, 1)
                    pe.wait_ge(hot_ready, 1)
                    for x in range(2 * TT):
                        i = nc.tensor.matmul(ps[:, 3, 0:2 * NBLK], slot_hot[:, x, :],
                                             row_hot[:, x].rearrange("p c b -> p (c b)"), start=x == 0,
                                             stop=x == 2 * TT - 1)
                    i.then_inc(table_made, 1)

                    def turn(x, group, count):
                        if not isinstance(count, int) or count > 2:
                            pe.wait_ge(e_t_tails, count - 2)
                        for k in range(4):
                            j, q = 2 * group + k // 2, k % 2
                            i = nc.tensor.transpose(ps[:, 6 + group, k * P:(k + 1) * P],
                                                    x[:, 256 * j + q:256 * j + 256:2], ident)
                        i.then_inc(e_turned, 1)

                    acts = act_rows[:].rearrange("p a b -> p (a b)")

                    def e_products(j, ring, count, bank, sh, st):
                        pe.wait_ge(e_tails, count + NER)
                        wh, wt = e_head[ring], e_tail[ring]
                        for q in range(2):
                            kk = 2 * j + q
                            start, stop = kk == 0, kk == KD - 1
                            for n in range(2):
                                o, cols = ps[:, bank + n, :], slice(n * 512, n * 512 + 512)
                                nc.tensor.matmul(o, sh[:, kk, :], wh[:, q, cols], start=start, stop=False)
                                nc.tensor.matmul(o, sh[:, kk, :], wt[:, q, cols], start=False, stop=False)
                            for n in range(2):
                                o, cols = ps[:, bank + n, :], slice(n * 512, n * 512 + 512)
                                i = nc.tensor.matmul(o, st[:, kk, :], wh[:, q, cols], start=False, stop=stop)
                        i.then_inc(e_used, 1)

                    def up(j, ring, count):
                        e_products(j % 4, ring, count, 0 if j < 4 else 2, xT_head, xT_tail)

                    def down(i, j, count):
                        if j == 0:
                            pe.wait_ge(out_moved, i)
                            pe.wait_ge(e_t_tails, 4 * i + 1)
                        if j == 2:
                            pe.wait_ge(e_t_tails, 4 * i + 2)
                        e_products(j, (8 + 8 + j) % NEH, count, 4, aT_head, aT_tail)

                    def body(i):
                        base = 12 * i - 4
                        pe.wait_ge(e_t_tails, 4 * i)
                        pe.wait_ge(sig_times, i)
                        up(0, 8 % NEH, base + 1)
                        pe.wait_ge(gated, i)
                        turn(acts, 0, 4 * i + 1)
                        up(1, 9 % NEH, base + 2)
                        turn(acts, 1, 4 * i + 2)
                        for j in range(2, 8):
                            up(j, (8 + j) % NEH, base + j + 1)
                        for j in range(4):
                            down(i, j, base + 8 + j + 1)
                            if j == 0:
                                pe.wait_ge(x_in, 16 * i + 32)
                            if j < 2:
                                turn(x_rows, j, 4 * i + 3 + j)

                    pe.sem_inc(e_used, NEH)
                    pe.wait_ge(x_in, 16)
                    turn(x_rows, 0, 1)
                    turn(x_rows, 1, 2)
                    pe.wait_ge(e_t_tails, 2)
                    for j in range(8):
                        up(j, j % NEH, j + 1)
                    pe.wait_ge(x_in, 32)
                    turn(x_rows, 0, 3)
                    turn(x_rows, 1, 4)
                    body(1)
                    pe.wait_ge(blocks_ready, 1)
                    n = pe.value_load(block_i[0:1, NBLK:NBLK + 1], min_val=E, max_val=E + OVF)
                    with pe.Fori(2, n) as i:
                        body(i)
                    last = pe.value_load(block_i[0:1, NBLK + 1:NBLK + 2], min_val=E - 1, max_val=E + OVF - 1)
                    pe.wait_ge(gated, last + 1)
                    turn(acts, 0, 4 * last + 5)
                    turn(acts, 1, 4 * last + 6)
                    for j in range(4):
                        if j == 0:
                            pe.wait_ge(out_moved, last + 1)
                            pe.wait_ge(e_t_tails, 4 * last + 6)
                        e_products(j, (8 + j) % NEH, 12 * last + 8 + j + 1, 4, aT_head, aT_tail)

            with nc.Block() as block:
                @block.sync
                def _(sp):
                    for t in range(TT):
                        sp.dma_start(rows1[:, t, :], y_rows[t * P:(t + 1) * P, :]).then_inc(y1_in[t], 16)
                        sp.dma_start(rows2[:, t, :], y_rows[T + t * P:T + (t + 1) * P, :]).then_inc(y2_in[t], 16)
                    for t in range(TT):
                        sp.wait_ge(norm2.ready, t + 1)
                        sp.dma_start(out_tiles[:, t, :], h[:, t, :]).then_inc(h_stored, 16)
                    sp.wait_ge(h_stored, 16 * TT)

                @block.scalar
                def _(act):
                    for t in range(TT):
                        for c in range(2):
                            i = act.activation(diag[:, t, c, :], const("ident"), ACT.Copy, scale=share[:, c, t:t + 1])
                        i.then_inc(diag_made, 1)
                    start2.scalar_chunk(act)
                    norm2.scalar(act, const("eps")[:, 0:1])
                    start2.scalar(act)

                @block.tensor
                def _(pe):
                    for t in range(TT):
                        pe.wait_ge(diag_made, t + 1)
                        for c, (rows, landed) in enumerate(((rows1, y1_in), (rows2, y2_in))):
                            pe.wait_ge(landed[t], 16)
                            for n in range(2):
                                i = nc.tensor.matmul(ps[:, 2 * t + n, :], diag[:, t, c, :],
                                                     rows[:, t, n * 512:n * 512 + 512], start=c == 0, stop=c == 1)
                        i.then_inc(y_summed, 1)
                    start2.tensor(pe)

                @block.gpsimd
                def _(pool):
                    start2.gpsimd(pool)
                    norm2.gpsimd(pool, ln2_gb[:, 1, :])

                @block.vector
                def _(v):
                    def add_experts(v, order, t):
                        v.wait_ge(y_summed, t + 1)
                        order.then(v.scalar_tensor_tensor(out=h[:, t, :], in0=h[:, t, :], scalar=ALPHA,
                                                          in1=ps[:, 2 * t:2 * t + 2, :].rearrange("p a b -> p (a b)"),
                                                          op0=ALU.mult, op1=ALU.add))

                    norm2.vector(v, Steps(v, c_order), add_experts, ln2_gb[:, 0, :], start2.vector)

            nc.gpsimd.dma_reset(range(sems[first_layer_sem].num, sems[-1].num + 1))
            nc.gpsimd.sem_clear(range(sems[first_layer_sem].num, sems[-1].num + 1))
            nc.all_engine_barrier()


INPUTS = ["x", "positions", "ln_in_g", "ln_in_b", "w_in", "conv_w", "sgu_ln_g", "sgu_ln_b", "w_s", "b_s",
          "lambda_q1", "lambda_k1", "lambda_q2", "lambda_k2", "diff_subln_g", "w_gate", "b_gate", "w_branch", "w_o",
          "ln1_g", "ln1_b", "w_router", "b_router", "w1", "w3", "w2", "ln2_g", "ln2_b"]


def kernel(**inputs):
    import concourse.bacc as bacc
    from concourse.bass_utils import run_bass_kernel_spmd

    nc = bacc.Bacc("TRN2", target_bir_lowering=False, num_devices=1)
    arrays = {name: np.ascontiguousarray(inputs[name]) for name in INPUTS}
    arrays["consts"], arrays["causal"], arrays["decay"], arrays["dispatch"] = constants()
    a = {name: nc.dram_tensor(f"in_{name}", x.shape, mybir.dt.from_np(x.dtype), kind="ExternalInput").ap()
         for name, x in arrays.items()}
    for name, shape, dt in (("h1_rows", (T, D), F32), ("y_rows", (2 * T, D), F32),
                            ("tables", (P, 5, T), F32)):
        a[name] = nc.dram_tensor(name, shape, dt).ap()
    out = nc.dram_tensor("out", (1, T, D), F32, kind="ExternalOutput").ap()
    program(nc, a, out)
    r = run_bass_kernel_spmd(nc, [{f"in_{name}": x for name, x in arrays.items()}], core_ids=[0])
    return r.results[0]["out"]
```
